# Optimizing a Trainium2 kernel written in Bass

```python
import jax, jax.numpy as jnp
from jax import lax
import numpy as np

D_MODEL = 1024
BATCH = 1
SEQ = 4096
DEPTH = 1
DEC_BATCH = 1
DEC_SEQ = 64
PAST_LEN = 512

CHUNK = 64
GROUP_W = D_MODEL // 4
D_MIX = 4 * GROUP_W
N_SPLITS = 11
IN_COLS = N_SPLITS * GROUP_W
CONV_A_W = 3
CONV_B_W = 31
POOL_WINDOWS = (2, 4, 8, 16)
POOL_GROUPS = len(POOL_WINDOWS)
POOL_CH = GROUP_W // POOL_GROUPS
POOL_HIST = max(POOL_WINDOWS) - 1
N_MEM = 256
MEM_HEADS = 4
MEM_HEAD_DIM = GROUP_W // MEM_HEADS
EPS = 1e-6

kernel_name = 'hymba_conv_pool_memory_streaming_encoder'

def _rmsnorm(x, g):
    xf = x.astype(jnp.float32)
    return (xf * lax.rsqrt(jnp.mean(xf * xf, axis=-1, keepdims=True) + EPS) * g.astype(jnp.float32)).astype(x.dtype)

def _layernorm(x, g, b):
    xf = x.astype(jnp.float32)
    mu = jnp.mean(xf, axis=-1, keepdims=True)
    xc = xf - mu
    var = jnp.mean(xc * xc, axis=-1, keepdims=True)
    return (xc * lax.rsqrt(var + EPS) * g.astype(jnp.float32) + b.astype(jnp.float32)).astype(x.dtype)

def _dwconv(xpad, w):
    c = xpad.shape[-1]
    return lax.conv_general_dilated(xpad, w[:, None, :].astype(xpad.dtype), window_strides=(1,), padding='VALID',
                                    dimension_numbers=('NWC', 'WIO', 'NWC'), feature_group_count=c)

def _multiscale_trailing_mean(ppad, pos0):
    t = ppad.shape[1] - POOL_HIST
    cs = lax.cumsum(ppad.astype(jnp.float32), axis=1)
    cs = jnp.concatenate([jnp.zeros_like(cs[:, :1]), cs], axis=1)
    pos = pos0 + jnp.arange(t)
    outs = []
    for gi, w in enumerate(POOL_WINDOWS):
        sl = slice(gi * POOL_CH, (gi + 1) * POOL_CH)
        end = cs[:, POOL_HIST + 1:POOL_HIST + 1 + t, sl]
        start = cs[:, POOL_HIST + 1 - w:POOL_HIST + 1 - w + t, sl]
        cnt = jnp.minimum(w, pos + 1).astype(jnp.float32)[None, :, None]
        outs.append((end - start) / cnt)
    return jnp.concatenate(outs, axis=-1)

def _mem_kv(mem, g, w_k, w_v):
    b = mem.shape[0]
    mn = _rmsnorm(mem, g)
    k = jnp.einsum('bmd,de->bme', mn, w_k).reshape(b, N_MEM, MEM_HEADS, MEM_HEAD_DIM)
    v = jnp.einsum('bmd,de->bme', mn, w_v).reshape(b, N_MEM, MEM_HEADS, MEM_HEAD_DIM)
    return k, v

def _layer(x, hist_a, hist_b, hist_p, mem_k, mem_v, pos0, lp):
    norm_g, w_in, conv_a_w, conv_b_w, conv_b_bias, ln_b_g, ln_b_b, pool_w, pool_bias, pool_scale, w_out = lp
    b, t, _ = x.shape
    h = _rmsnorm(x, norm_g)
    u = jnp.einsum('btd,de->bte', h, w_in)
    a_b, a_c, a_x, a_g, b_v, b_a, b_g, c_u, c_g, x_q, x_g = jnp.split(u, N_SPLITS, axis=-1)

    v = a_c * a_x
    vpad = jnp.concatenate([hist_a, v], axis=1)
    y_a = a_b * _dwconv(vpad, conv_a_w) * jax.nn.silu(a_g)
    new_a = vpad[:, -(CONV_A_W - 1):]

    glu = b_v * jax.nn.sigmoid(b_a)
    gpad = jnp.concatenate([hist_b, glu], axis=1)
    z = _dwconv(gpad, conv_b_w) + conv_b_bias
    z = _layernorm(z, ln_b_g, ln_b_b)
    y_b = jax.nn.silu(z) * jax.nn.silu(b_g)
    new_b = gpad[:, -(CONV_B_W - 1):]

    ppad = jnp.concatenate([hist_p, c_u], axis=1)
    pooled = _multiscale_trailing_mean(ppad, pos0)
    d = (pooled - c_u.astype(jnp.float32)).astype(c_u.dtype).reshape(b, t, POOL_GROUPS, POOL_CH)
    mixed = jnp.einsum('btgc,gce->btge', d, pool_w).reshape(b, t, GROUP_W) + pool_bias
    y_c = mixed * pool_scale * jax.nn.silu(c_g)
    new_p = ppad[:, -POOL_HIST:]

    q = x_q.reshape(b, t, MEM_HEADS, MEM_HEAD_DIM)
    s = jnp.einsum('bthd,bmhd->bhtm', q, mem_k).astype(jnp.float32) * (MEM_HEAD_DIM ** -0.5)
    p = jax.nn.softmax(s, axis=-1).astype(mem_v.dtype)
    o = jnp.einsum('bhtm,bmhd->bthd', p, mem_v).reshape(b, t, GROUP_W)
    y_x = o * jax.nn.silu(x_g)

    y = jnp.concatenate([y_a, y_b, y_c, y_x], axis=-1)
    return x + jnp.einsum('bte,ed->btd', y, w_out), new_a, new_b, new_p

def setup_inputs(seed: int = 0) -> dict:
    key = jax.random.key(seed)
    ks = jax.random.split(key, 24)
    f = jnp.float32
    nrm = lambda k, shape, scale: jax.random.normal(k, shape, f) * scale
    return {
        'x_prompt': nrm(ks[0], (BATCH, SEQ, D_MODEL), 1.0),
        'x_sample': nrm(ks[1], (DEC_BATCH, DEC_SEQ, D_MODEL), 1.0),
        'mem_prompt': nrm(ks[2], (BATCH, N_MEM, D_MODEL), 1.0),
        'state_conv_a': nrm(ks[3], (DEPTH, DEC_BATCH, CONV_A_W - 1, GROUP_W), 1.0),
        'state_conv_b': nrm(ks[4], (DEPTH, DEC_BATCH, CONV_B_W - 1, GROUP_W), 1.0),
        'state_pool': nrm(ks[5], (DEPTH, DEC_BATCH, POOL_HIST, GROUP_W), 1.0),
        'cache_mem_k': nrm(ks[6], (DEPTH, DEC_BATCH, N_MEM, MEM_HEADS, MEM_HEAD_DIM), 1.0),
        'cache_mem_v': nrm(ks[7], (DEPTH, DEC_BATCH, N_MEM, MEM_HEADS, MEM_HEAD_DIM), 1.0),
        'norm_g': 1.0 + nrm(ks[8], (DEPTH, D_MODEL), 0.05),
        'w_in': nrm(ks[9], (DEPTH, D_MODEL, IN_COLS), D_MODEL ** -0.5),
        'conv_a_w': nrm(ks[10], (DEPTH, CONV_A_W, GROUP_W), CONV_A_W ** -0.5),
        'conv_b_w': nrm(ks[11], (DEPTH, CONV_B_W, GROUP_W), CONV_B_W ** -0.5),
        'conv_b_bias': nrm(ks[12], (DEPTH, GROUP_W), 0.02),
        'ln_b_g': 1.0 + nrm(ks[13], (DEPTH, GROUP_W), 0.05),
        'ln_b_b': nrm(ks[14], (DEPTH, GROUP_W), 0.02),
        'pool_w': nrm(ks[15], (DEPTH, POOL_GROUPS, POOL_CH, POOL_CH), POOL_CH ** -0.5),
        'pool_bias': nrm(ks[16], (DEPTH, GROUP_W), 0.02),
        'pool_scale': 1.0 + nrm(ks[17], (DEPTH, GROUP_W), 0.1),
        'mem_norm_g': 1.0 + nrm(ks[18], (DEPTH, D_MODEL), 0.05),
        'w_mem_k': nrm(ks[19], (DEPTH, D_MODEL, GROUP_W), D_MODEL ** -0.5),
        'w_mem_v': nrm(ks[20], (DEPTH, D_MODEL, GROUP_W), D_MODEL ** -0.5),
        'w_out': nrm(ks[21], (DEPTH, D_MIX, D_MODEL), D_MIX ** -0.5),
        'final_norm_g': 1.0 + nrm(ks[22], (D_MODEL,), 0.05),
    }

def reference(x_prompt, x_sample, mem_prompt, state_conv_a, state_conv_b, state_pool, cache_mem_k, cache_mem_v,
              norm_g, w_in, conv_a_w, conv_b_w, conv_b_bias, ln_b_g, ln_b_b, pool_w, pool_bias, pool_scale,
              mem_norm_g, w_mem_k, w_mem_v, w_out, final_norm_g):
    xp, xs = x_prompt, x_sample
    bp = xp.shape[0]
    na_p, nb_p, np_p, mk_p, mv_p = [], [], [], [], []
    na_s, nb_s, np_s = [], [], []
    for l in range(DEPTH):
        lp = (norm_g[l], w_in[l], conv_a_w[l], conv_b_w[l], conv_b_bias[l], ln_b_g[l], ln_b_b[l],
              pool_w[l], pool_bias[l], pool_scale[l], w_out[l])
        mk, mv = _mem_kv(mem_prompt, mem_norm_g[l], w_mem_k[l], w_mem_v[l])
        za = jnp.zeros((bp, CONV_A_W - 1, GROUP_W), xp.dtype)
        zb = jnp.zeros((bp, CONV_B_W - 1, GROUP_W), xp.dtype)
        zp = jnp.zeros((bp, POOL_HIST, GROUP_W), xp.dtype)
        xp, a1, b1, p1 = _layer(xp, za, zb, zp, mk, mv, 0, lp)
        na_p.append(a1); nb_p.append(b1); np_p.append(p1); mk_p.append(mk); mv_p.append(mv)
        xs, a2, b2, p2 = _layer(xs, state_conv_a[l], state_conv_b[l], state_pool[l],
                                cache_mem_k[l], cache_mem_v[l], PAST_LEN, lp)
        na_s.append(a2); nb_s.append(b2); np_s.append(p2)
    y_prompt = _rmsnorm(xp, final_norm_g)
    y_sample = _rmsnorm(xs, final_norm_g)
    return (y_prompt, y_sample,
            jnp.stack(na_p), jnp.stack(nb_p), jnp.stack(np_p), jnp.stack(mk_p), jnp.stack(mv_p),
            jnp.stack(na_s), jnp.stack(nb_s), jnp.stack(np_s))


_drawn_inputs = setup_inputs


def setup_inputs(seed=0):
    import zlib

    import numpy as np

    out = dict(_drawn_inputs(seed))
    spreads = {}
    factors = {'state_pool': 2.917,
     'conv_b_bias': 8.0,
     'ln_b_g': 5.349,
     'ln_b_b': 21.346,
     'pool_bias': 8.0,
     'state_conv_a': 2.729,
     'cache_mem_k': 3.6,
     'cache_mem_v': 2.778,
     'pool_scale': 3.488}
    for name, (base, spread) in spreads.items():
        noise = np.random.default_rng([zlib.crc32(name.encode()), seed]).standard_normal(out[name].shape)
        drawn = base * np.exp(spread * noise) if base else spread * noise
        out[name] = __import__('jax').numpy.asarray(drawn.astype(out[name].dtype))
    for name, factor in factors.items():
        out[name] = (out[name] * factor).astype(out[name].dtype)
    return out
```

```python
from contextlib import ExitStack

import concourse.bass as bass
from concourse import mybir

F32 = mybir.dt.float32
F32R = mybir.dt.float32r
F16 = mybir.dt.float16
BF16 = mybir.dt.bfloat16
I32 = mybir.dt.int32
ACT = mybir.ActivationFunctionType
ALU = mybir.AluOpType
AX = mybir.AxisListType

P = 128
D = 1024
KT = D // P
GW = 256
CT = GW // P
NG = 11
FT = NG * CT
SEQ, SAMPLE = 4096, 64
N = 256
CHUNKS = SEQ // N
LAST = CHUNKS - 1
TA, TB, HP = 3, 31, 15
HA, HB = TA - 1, TB - 1
HEADS, HD, NMEM = 4, 64, 256
PAIRS, MT = HEADS // 2, NMEM // P
WINDOWS = (2, 4, 8, 16)
EPS = 1e-6
HALF = 512

SPLIT = {"a_b": 0, "a_c": 1, "a_x": 2, "a_g": 3, "b_v": 4, "b_a": 5, "b_g": 6, "c_u": 7, "c_g": 8,
         "x_q": 9, "x_g": 10}
ORDER = ["b_a", "b_v", "x_q", "c_u", "a_c", "a_x", "a_b", "a_g", "b_g", "c_g", "x_g"]

SLOTS = ["b_a", "b_v", "x_q", "c_u", "a_c", "a_x", "a_b", "a_g", "mix", "b_g", "zf", "c_g", "x_g",
         "zb", "t0", "t1", "t2", "t3"]
PREP = [f"w{j}" for j in range(FT)]
FIRST = ["m0", "m1", "m2", "m3", "t0", "t1", "t2", "t3"] + PREP[:4]
for _n, _g in enumerate(ORDER):
    FIRST += {"b_g": ["mix"], "c_g": ["zf"]}.get(_g, []) + [_g] + PREP[4 + 2 * _n:6 + 2 * _n]
FIRST += ["zb", "n0", "n1", "n2", "n3"]
NFIRST = len(FIRST)

Y_ORDER = [0, 4, 6, 2]
K_ORDER = [k + c for k in Y_ORDER for c in range(CT)]
PIECES = 2 * KT
RAW, WST = 4, 4

R_AW, R_BW = 0, TA
R_BIAS, R_LNG, R_LNB, R_PB, R_PS = range(TA + TB, TA + TB + 5)
NR = TA + TB + 5

MAGIC = 0x5F3759DF
NEWTON = 3
XSCALE = 1024.0
WEXP = 14


def encoder_program(nc, x_prompt, x_sample, mem_prompt, state_conv_a, state_conv_b, state_pool,
                    cache_mem_k, cache_mem_v, norm_g, w_in, conv_a_w, conv_b_w, conv_b_bias, ln_b_g,
                    ln_b_b, pool_w, pool_bias, pool_scale, mem_norm_g, w_mem_k, w_mem_v, w_out,
                    final_norm_g, y_prompt, y_sample, new_a_p, new_b_p, new_c_p, new_k, new_v,
                    new_a_s, new_b_s, new_c_s):
    ctx = ExitStack()
    with ctx:
        def sb(name, shape, dt=F32):
            return ctx.enter_context(nc.sbuf_tensor(name, shape, dt))

        def sem(name):
            return ctx.enter_context(nc.semaphore(name))

        w_hi = sb("w_hi", [P, FT, KT, P], F16)
        w_lo = sb("w_lo", [P, FT, KT, P], F16)
        stage = sb("stage", [P, 2, KT, P])
        raw = stage[:, :, :, :].rearrange("p a b c -> p (a b c)").rearrange("p (s n) -> p s n", n=HALF)
        wo_hi = sb("wo_hi", [P, WST, HALF], F32R)
        wo_lo = sb("wo_lo", [P, WST, HALF], F32R)
        h_hi = sb("h_hi", [P, KT, N], F16)
        h_lo = sb("h_lo", [P, KT, N], F16)
        y_hi = sb("y_hi", [P, KT, N], F32R)
        y_lo = sb("y_lo", [P, KT, N], F32R)
        xb = sb("xb", [P, D])
        ob = sb("ob", [P, 2, D])
        kt_hi = sb("kt_hi", [P, PAIRS, NMEM], F32R)
        kt_lo = sb("kt_lo", [P, PAIRS, NMEM], F32R)
        v_hi = sb("v_hi", [P, MT, PAIRS, 3 * HD], F32R)
        v_lo = sb("v_lo", [P, MT, PAIRS, 3 * HD], F32R)
        probs = sb("probs", [P, 2, 2, NMEM])
        kv = probs[:, :, :, :].rearrange("p b h m -> p b (h m)")
        pt_hi = sb("pt_hi", [P, 2, MT, N], F32R)
        pt_lo = sb("pt_lo", [P, 2, MT, N], F32R)
        glu = sb("glu", [P, CT, HB + N])
        va = sb("va", [P, CT, HA + N])
        cu = sb("cu", [P, CT, HP + N])
        z = sb("z", [P, CT, N])
        ya = sb("ya", [P, CT, N])
        yc = sb("yc", [P, CT, N])
        gate = sb("gate", [P, 3, CT, N])
        dq_hi = sb("dq_hi", [P, CT, N], F32R)
        dq_lo = sb("dq_lo", [P, CT, N], F32R)
        S2, S4 = HP - 1, HP - 3
        sa = sb("sa", [P, CT, S2 + N])
        sb_ = sb("sb4", [P, CT, S4 + N])
        zt = sa[:, :, :].rearrange("p a b -> p (a b)")[:, 0:2 * GW].rearrange("p (t c) -> p t c", t=2)
        junk = sb("junk", [P, D], BF16)
        pw_hi = sb("pw_hi", [P, CT, P], F32R)
        pw_lo = sb("pw_lo", [P, CT, P], F32R)
        gf = sb("gf", [P, D])
        l1 = gf[:, 0:3 * P].rearrange("p (s n) -> p s n", s=3)
        mags = gf[:, 3 * P:7 * P].bitcast(BF16).rearrange("p (k n) -> p k n", n=P)
        ident = sb("ident", [P, P])
        ones = sb("ones", [P, P], BF16)
        cst = sb("cst", [P, CT, NR])
        pbs = sb("pbs", [P, CT])
        gcol = sb("gcol", [P, 2 * KT])
        inv = sb("inv", [P, FT])
        ramp = sb("ramp", [P, CT, 16])
        c15 = sb("c15", [P, 2])
        st = sb("st", [P, 96])
        (X_SQ, X_V, X_SH, X_Y, X_T), (O_SQ, O_V, O_SH, O_Y, O_T), (L_V, L_SH, L_Y, L_T) = (
            [st[:, 2 * (a + b):2 * (a + b) + 2] for b in range(m)] for a, m in ((0, 5), (5, 5), (10, 4)))
        nmax, rsum, rcp = (st[:, 28 + 8 * a:36 + 8 * a].rearrange("p (s h) -> p s h", h=2) for a in range(3))
        bn6 = st[:, 52:64].rearrange("p (t s) -> p t s", t=2)
        mv = st[:, 64:68].rearrange("p (t s) -> p t s", t=2)

        U = [ctx.enter_context(nc.psum_tensor(f"u{b}", [P, HALF], F32)) for b in range(3)]
        sps = ctx.enter_context(nc.psum_tensor("sps", [P, 2, HALF], F32))
        qps = ctx.enter_context(nc.psum_tensor("qps", [P, 2, HALF], F32))
        ops = ctx.enter_context(nc.psum_tensor("ops", [P, HALF], F32))

        class Signal:
            def __init__(self, name, per):
                self.sem, self.per = sem(name), per

            def at(self, i, k):
                return i * self.per + k

        def signal(name, per=1):
            return Signal(name, per)

        def needed(value):
            return type(value) is not int or value > 0

        c_in, ident_ok, consts_ok, ctr, cev, pw_in, pw_ok = (
            signal(n) for n in ("c_in", "ident_ok", "consts_ok", "ctr", "cev", "pw_in", "pw_ok"))
        ramp_s, zero_ok, gf_in = signal("ramp_s"), signal("zero_ok"), signal("gf_in")
        stage_in = [signal(f"stage_in{b}") for b in range(2)]
        wg_ok, mags_ok, l1_s, scaled, whi_ok, wlo_ok = (
            signal(n, 0) for n in ("wg_ok", "mags_ok", "l1_s", "scaled", "whi_ok", "wlo_ok"))
        kw_in = [signal(f"kw_in{b}") for b in range(4)]
        mn_hi, mn_lo, kw_hi, kw_lo, kvp, kv_ok, kv_in, ktp, kt_h, kt_l, v_h, v_l = (
            signal(n) for n in ("mn_hi", "mn_lo", "kw_hi", "kw_lo", "kvp", "kv_ok", "kv_in", "ktp",
                                "kt_h", "kt_l", "v_h", "v_l"))
        st_in, stp, st_ok, stored_st = (signal(n) for n in ("st_in", "stp", "st_ok", "stored_st"))
        x_in = signal("x_in", 32)
        x_sq, x_v, x_newton, x_scaled = signal("x_sq", 2), signal("x_v", 8), signal("x_newton", 8 * NEWTON), signal("x_scaled", 2)
        h_hi_ok, h_lo_ok = signal("h_hi_ok", 4), signal("h_lo_ok", 4)
        u_ready = signal("u_ready", len(SLOTS))
        s_ready, pt_ready, pv_ready, o_piece = signal("s_ready", 2), signal("pt_ready", 2), signal("pv_ready", 2), signal("o_piece", PIECES)
        hist_ok, sig_ok, glu_ok, conv_step = signal("hist_ok", 3), signal("sig_ok"), signal("glu_ok"), signal("conv_step", 2 * TB)
        bn_s, ln_v, ln_newton, zt_ok, zs_ok, bg_ok, yb_ok = (
            signal("bn_s", 2), signal("ln_v", 4), signal("ln_newton", 4 * NEWTON), signal("zt_ok"),
            signal("zs_ok"), signal("bg_ok"), signal("yb_ok"))
        ac_ok, va_ok, conv_a, ag_ok, ya_ok = signal("ac_ok"), signal("va_ok"), signal("conv_a", 4 * CT), signal("ag_ok"), signal("ya_ok")
        cu_ok, win_ok, d_ok, d_hi, d_lo, mix_ok, cg_ok, yc_ok = (
            signal("cu_ok"), signal("win_ok", 4), signal("d_ok"), signal("d_hi"), signal("d_lo"),
            signal("mix_ok"), signal("cg_ok"), signal("yc_ok"))
        q_hi, q_lo, nmax_ok, exp_ok, rcp_ok, p_ok = (
            signal("q_hi"), signal("q_lo"), signal("nmax_ok", 2), signal("exp_ok", 4), signal("rcp_ok", 4), signal("p_ok", 4))
        pt_hi_ok, pt_lo_ok, xg_ok, yx_ok = signal("pt_hi_ok", 4), signal("pt_lo_ok", 4), signal("xg_ok"), signal("yx_ok")
        y_hi_ok, y_lo_ok = signal("y_hi_ok", 4), signal("y_lo_ok", 4)
        raw_in = [signal(f"raw_in{b}", 16 * PIECES // RAW) for b in range(RAW)]
        wo_hi_ok, wo_lo_ok = signal("wo_hi_ok", PIECES), signal("wo_lo_ok", PIECES)
        res_in, stored = [signal(f"res_in{t}", 16) for t in range(2)], [signal(f"stored{t}", 16) for t in range(2)]
        r_ok, o_sq, o_v, o_newton, o_rs, o_ok = (
            signal("r_ok", 4), signal("o_sq", 2), signal("o_v", 4), signal("o_newton", 4 * NEWTON),
            signal("o_rs"), signal("o_ok"))

        def slot(i, name):
            if type(i) is int and i == 0:
                n = FIRST.index(name)
                return n + 1, U[n % 3]
            if name == "w":
                return None
            k = SLOTS.index(name)
            if type(i) is int and i == CHUNKS:
                return NFIRST + len(SLOTS) * (CHUNKS - 1) - 2 + k + 1, U[(NFIRST - 2 + k) % 3]
            return (i - 1) * len(SLOTS) + NFIRST + k + 1, U[(NFIRST + k) % 3]

        EMPTIED = {"b_a": (sig_ok, 1), "b_v": (glu_ok, 1), "x_q": (q_lo, 1), "c_u": (cu_ok, 1),
                   "a_c": (ac_ok, 1), "a_x": (va_ok, 1), "a_b": (conv_a, 4 * CT), "a_g": (ag_ok, 1),
                   "mix": (mix_ok, 1), "b_g": (bg_ok, 1), "zf": (zt_ok, 1), "c_g": (cg_ok, 1),
                   "x_g": (xg_ok, 1), "zb": (zs_ok, 1)}
        EMPTIED |= {f"m{j}": (mn_lo, j + 1) for j in range(4)}
        EMPTIED |= {f"w{j}": (l1_s, 5 * j + 1) for j in range(FT)}

        def emptied(i, name):
            if type(i) is int and i == 0:
                n = FIRST.index(name) - 3
                if n < 0:
                    return None
                name, j = FIRST[n], 0
                if name[0] == "n":
                    name, j = "t" + name[1], 1
            else:
                k = SLOTS.index(name)
                order = SLOTS[:-2] if type(i) is int and i == CHUNKS else SLOTS
                if k >= 3:
                    name, j = SLOTS[k - 3], i + (SLOTS[k - 3] in ("t0", "t1", "t2", "t3"))
                else:
                    name = order[k - 3]
                    j = i if name[0] == "t" else i - 1
            if name[0] == "t" and name[1:].isdigit():
                return h_lo_ok.sem, h_lo_ok.at(j, int(name[1]) + 1)
            s, c = EMPTIED[name]
            return s.sem, s.at(j, c)

        def tiles(n):
            return [(t, t * P, min(P, n - t * P)) for t in range((n + P - 1) // P)]

        w_in_v = w_in[0].rearrange("(k p) (f c) -> f p k c", p=P, c=P)
        w_out_v = w_out[0].rearrange("(k p) (h c) -> h k p c", p=P, c=HALF)
        PREP_FT = [SPLIT[g] * CT + c for g in ORDER for c in range(CT)]

        block = ctx.enter_context(nc.Block())

        @block.sync
        def _(sp):
            sp.dma_start(z[0:TA, 0, :], conv_a_w[0]).then_inc(c_in.sem, 16)
            sp.dma_start(z[R_BW:R_BW + TB, 0, :], conv_b_w[0]).then_inc(c_in.sem, 16)
            for r, v in ((R_BIAS, conv_b_bias), (R_LNG, ln_b_g), (R_LNB, ln_b_b), (R_PB, pool_bias), (R_PS, pool_scale)):
                sp.dma_start(z[r:r + 1, 0, :], v).then_inc(c_in.sem, 16)
            sp.dma_start(z[0:KT, 1, 0:P], norm_g[0].rearrange("(k p) -> k p", p=P)).then_inc(c_in.sem, 16)
            sp.dma_start(z[KT:2 * KT, 1, 0:P], mem_norm_g[0].rearrange("(k p) -> k p", p=P)).then_inc(c_in.sem, 16)
            sp.dma_start(xb[:, :], mem_prompt[0, 0:P, :]).then_inc(x_in.sem, 16)
            sp.dma_start(stage[:, 0], w_in_v[PREP_FT[0]]).then_inc(stage_in[0].sem, 16)
            sp.dma_start(stage[:, 1], w_in_v[PREP_FT[1]]).then_inc(stage_in[1].sem, 16)

            def load_memory_weights(k):
                if k >= 4:
                    sp.wait_ge(kw_lo.sem, k - 3)
                b = k % 4
                dst = ob[:, b // 2, (b % 2) * HALF:(b % 2 + 1) * HALF]
                sp.dma_start(dst[:, 0:GW], w_mem_k[0, k * P:(k + 1) * P, :]).then_inc(kw_in[b].sem, 16)
                sp.dma_start(dst[:, GW:2 * GW], w_mem_v[0, k * P:(k + 1) * P, :]).then_inc(kw_in[b].sem, 16)

            for k in range(4):
                load_memory_weights(k)
            sp.wait_ge(zero_ok.sem, 1)
            for g in range(4):
                q = (g % 2) * HD
                sp.dma_start(ya[q:q + HD, 0, (g // 2) * P + q:(g // 2) * P + q + HD], pool_w[0, g]).then_inc(pw_in.sem, 16)

            sp.wait_ge(u_ready.sem, FIRST.index("m1") + 1)
            sp.dma_start(xb[:, :], mem_prompt[0, P:2 * P, :]).then_inc(x_in.sem, 16)
            for k in range(4, KT):
                load_memory_weights(k)
            sp.wait_ge(u_ready.sem, FIRST.index("m3") + 1)
            sp.dma_start(xb[:, :], x_prompt[0, 0:P, :]).then_inc(x_in.sem, 16)
            sp.wait_ge(u_ready.sem, FIRST.index("t1") + 1)
            sp.dma_start(xb[:, :], x_prompt[0, P:2 * P, :]).then_inc(x_in.sem, 16)
            for j in range(2, FT):
                sp.wait_ge(wlo_ok.sem, j - 1)
                sp.dma_start(stage[:, j % 2], w_in_v[PREP_FT[j]]).then_inc(stage_in[j % 2].sem, 16)
                if j == 3:
                    sp.wait_ge(u_ready.sem, FIRST.index("t3") + 1)
                    sp.dma_start(xb[:, :], x_prompt[0, 2 * P:3 * P, :]).then_inc(x_in.sem, 16)
                if j == 4:
                    sp.wait_ge(kv_ok.sem, 2)
                    for src, off in ((new_k, 0), (new_v, GW)):
                        sp.dma_start(src[0, 0].rearrange("(t p) h d -> p t (h d)", p=P), kv[:, :, off:off + GW]).then_inc(kv_in.sem, 16)

            def sync_chunk(i, n, x_here, y_here, x_next, x_after):
                for t, _, m in tiles(n):
                    if type(i) is int and i == 0:
                        sp.wait_ge(kw_lo.sem, KT)
                    else:
                        sp.wait_ge(stored[t].sem, stored[t].at(i, 0))
                    sp.dma_start(ob[0:m, t, :], x_here[t]).then_inc(res_in[t].sem, 16)
                for q in range(PIECES):
                    if q < RAW and type(i) is int and i == 0:
                        if q == 0:
                            sp.wait_ge(wlo_ok.sem, FT)
                            sp.dma_start(gf[:, :], final_norm_g.partition_broadcast(P)).then_inc(gf_in.sem, 16)
                    else:
                        sp.wait_ge(wo_lo_ok.sem, wo_lo_ok.at(i, q - RAW + 1))
                    half, k = q // KT, K_ORDER[q % KT]
                    sp.dma_start(raw[:, q % RAW, :], w_out_v[half, k]).then_inc(raw_in[q % RAW].sem, 16)
                    if q == 4 and x_next is not None:
                        v = NFIRST - 2 if type(i) is int and i == 0 else i * len(SLOTS) + NFIRST - 2
                        sp.wait_ge(u_ready.sem, v)
                        sp.dma_start(xb[:, :], x_next).then_inc(x_in.sem, 16)
                if x_after is not None:
                    sp.wait_ge(u_ready.sem, i * len(SLOTS) + NFIRST)
                    sp.dma_start(xb[0:x_after.shape[0], :], x_after).then_inc(x_in.sem, 16)
                sp.wait_ge(o_ok.sem, o_ok.at(i, 1))
                for t, _, m in tiles(n):
                    sp.dma_start(y_here[t], ob[0:m, t, :]).then_inc(stored[t].sem, 16)

            def prompt_chunk(i, here, nxt, after):
                sync_chunk(i, N, [x_prompt[0, bass.ds(h, P), :] for h in here], [y_prompt[0, bass.ds(h, P), :] for h in here],
                           x_prompt[0, bass.ds(nxt, P), :] if nxt is not None else None,
                           x_prompt[0, bass.ds(after, P), :] if after is not None else x_sample[0] if nxt is not None else None)

            prompt_chunk(0, [0, P], N + P, 2 * N)
            with sp.Fori(1, LAST - 1) as i:
                h0, h1, nx, af = (sp.snap(i * N + t) for t in (0, P, N + P, 2 * N))
                prompt_chunk(i, [h0, h1], nx, af)
            prompt_chunk(LAST - 1, [(LAST - 1) * N, (LAST - 1) * N + P], LAST * N + P, None)
            prompt_chunk(LAST, [LAST * N, LAST * N + P], None, None)

            def load_sample_memory():
                sp.wait_ge(pt_ready.sem, pt_ready.at(LAST, 2))
                sp.dma_start(kv[:, :, 0:GW], cache_mem_k[0, 0].rearrange("(t p) h d -> p t (h d)", p=P)).then_inc(kv_in.sem, 16)
                sp.dma_start(kv[:, :, GW:2 * GW], cache_mem_v[0, 0].rearrange("(t p) h d -> p t (h d)", p=P)).then_inc(kv_in.sem, 16)

            def store_states(k, outs):
                sp.wait_ge(st_ok.sem, 2 * k + 2)
                (a, b, c) = outs
                sp.dma_start(b[0, 0], ya[0:HB, 0, :]).then_inc(stored_st.sem, 16)
                sp.dma_start(c[0, 0], ya[0:HP, 1, :]).then_inc(stored_st.sem, 16)
                sp.dma_start(a[0, 0], yc[0:HA, 0, :]).then_inc(stored_st.sem, 16)

            load_sample_memory()
            store_states(0, (new_a_p, new_b_p, new_c_p))
            sp.wait_ge(conv_step.sem, conv_step.at(LAST, 2 * TB))
            sp.wait_ge(zs_ok.sem, zs_ok.at(LAST, 1))
            sp.wait_ge(y_lo_ok.sem, y_lo_ok.at(LAST, 4))
            sp.dma_start(z[0:HB, 0, :], state_conv_b[0, 0]).then_inc(st_in.sem, 16)
            sp.dma_start(z[0:HP, 1, :], state_pool[0, 0]).then_inc(st_in.sem, 16)
            sp.wait_ge(stored_st.sem, 48)
            sp.dma_start(yc[0:HA, 1, :], state_conv_a[0, 0]).then_inc(st_in.sem, 16)
            sync_chunk(CHUNKS, SAMPLE, [x_sample[0, :, :]], [y_sample[0, :, :]], None, None)
            store_states(1, (new_a_s, new_b_s, new_c_s))
            sp.wait_ge(stored_st.sem, 96)
            sp.wait_ge(kv_in.sem, 64)
            sp.wait_ge(stored[0].sem, stored[0].at(CHUNKS + 1, 0))
            sp.wait_ge(stored[1].sem, stored[1].at(CHUNKS, 0))

        @block.tensor
        def _(pe):
            def three(out, a_hi, a_lo, b_hi, b_lo, first, last):
                nc.tensor.matmul(out, a_hi, b_hi, start=first, stop=False)
                nc.tensor.matmul(out, a_hi, b_lo, start=False, stop=False)
                return nc.tensor.matmul(out, a_lo, b_hi, start=False, stop=last)

            def transposes(i, names, j):
                m = j[1]
                pe.wait_ge(x_scaled.sem, j[0] + 1)
                for h, name in enumerate(names):
                    free = emptied(i, name)
                    if free:
                        pe.wait_ge(*free)
                    _, bank = slot(i, name)
                    for k in range(4):
                        c = (4 * h + k) * P
                        ins = nc.tensor.transpose(bank[:, k * P:k * P + m], xb[0:m, c:c + P], ident[0:m, 0:m])
                    ins.then_inc(u_ready.sem, 1)

            def weight_sums(j):
                free = emptied(0, f"w{j}")
                if free:
                    pe.wait_ge(*free)
                pe.wait_ge(mags_ok.sem, j + 1)
                _, bank = slot(0, f"w{j}")
                for k in range(KT):
                    ins = nc.tensor.matmul(bank[:, 0:P], ones[:, :], mags[:, k, :], start=k == 0, stop=k == KT - 1)
                ins.then_inc(u_ready.sem, 1)

            def project(i, n, name):
                free = emptied(i, name)
                if free:
                    pe.wait_ge(*free)
                _, bank = slot(i, name)
                g = SPLIT[name]
                if name == ORDER[0]:
                    pe.wait_ge(h_lo_ok.sem, h_lo_ok.at(i, 4 if n == N else 2))
                if type(i) is int and i == 0:
                    pe.wait_ge(wlo_ok.sem, 2 * ORDER.index(name) + 2)
                for c in range(CT):
                    for k in range(KT):
                        f = g * CT + c
                        ins = three(bank[:, c * N:c * N + n], w_hi[:, f, k, :], w_lo[:, f, k, :],
                                    h_hi[:, k, 0:n], h_lo[:, k, 0:n], k == 0, k == KT - 1)
                ins.then_inc(u_ready.sem, 1)

            def scores(i, n, p):
                nt = len(tiles(n))
                if p == 0:
                    pe.wait_ge(q_lo.sem, q_lo.at(i, 1))
                    if not (type(i) is int and i == 0):
                        pe.wait_ge(r_ok.sem, r_ok.at(i, -2))
                        if type(i) is int and i == CHUNKS:
                            pe.wait_ge(st_ok.sem, 2)
                else:
                    pe.wait_ge(exp_ok.sem, exp_ok.at(i, nt))
                for t, t0, m in tiles(n):
                    for h in range(2):
                        r = slice(h * HD, (h + 1) * HD)
                        ins = three(sps[0:m, h, t * NMEM:(t + 1) * NMEM], dq_hi[r, p, t0:t0 + m], dq_lo[r, p, t0:t0 + m],
                                    kt_hi[r, p, :], kt_lo[r, p, :], True, True)
                ins.then_inc(s_ready.sem, 1)

            def probs_t(i, n, p):
                nt = len(tiles(n))
                if p == 0:
                    if not (type(i) is int and i == 0):
                        pe.wait_ge(r_ok.sem, r_ok.at(i, 0))
                else:
                    pe.wait_ge(pt_lo_ok.sem, pt_lo_ok.at(i, 2))
                pe.wait_ge(p_ok.sem, p_ok.at(i, (p + 1) * nt))
                for t, t0, m in tiles(n):
                    b = (p * nt + t) % 2
                    for h in range(2):
                        for k in range(MT):
                            ins = nc.tensor.transpose(qps[:, h, k * N + t0:k * N + t0 + m],
                                                      probs[0:m, b, h, k * P:(k + 1) * P], ident[0:m, 0:m])
                ins.then_inc(pt_ready.sem, 1)

            def attend(i, n, p):
                if p == 0:
                    if needed(yx_ok.at(i, 0)):
                        pe.wait_ge(yx_ok.sem, yx_ok.at(i, 0))
                pe.wait_ge(pt_lo_ok.sem, pt_lo_ok.at(i, 2 * p + 2))
                for h in range(2):
                    for k in range(MT):
                        v = slice(h * HD, h * HD + P)
                        ins = three(ops[:, p * N:p * N + n], v_hi[:, k, p, v], v_lo[:, k, p, v],
                                    pt_hi[:, h, k, 0:n], pt_lo[:, h, k, 0:n],
                                    (h, k) == (0, 0), (h, k) == (1, MT - 1))
                ins.then_inc(pv_ready.sem, 1)

            def mix(i, n):
                free = emptied(i, "mix")
                if free:
                    pe.wait_ge(*free)
                _, bank = slot(i, "mix")
                pe.wait_ge(d_lo.sem, d_lo.at(i, 1))
                if type(i) is int and i == 0:
                    pe.wait_ge(pw_ok.sem, 2)
                for c in range(CT):
                    ins = three(bank[:, c * N:c * N + n], pw_hi[:, c, :], pw_lo[:, c, :],
                                dq_hi[:, c, 0:n], dq_lo[:, c, 0:n], True, True)
                ins.then_inc(u_ready.sem, 1)

            def z_rows(i, n):
                free = emptied(i, "zf")
                if free:
                    pe.wait_ge(*free)
                _, bank = slot(i, "zf")
                pe.wait_ge(conv_step.sem, conv_step.at(i, 2 * TB))
                for t, t0, m in tiles(n):
                    for c in range(CT):
                        ins = nc.tensor.transpose(bank[0:m, t * GW + c * P:t * GW + (c + 1) * P],
                                                  z[:, c, t0:t0 + m], ident[:, :])
                ins.then_inc(u_ready.sem, 1)

            def z_back(i, n):
                free = emptied(i, "zb")
                if free:
                    pe.wait_ge(*free)
                _, bank = slot(i, "zb")
                pe.wait_ge(zt_ok.sem, zt_ok.at(i, 1))
                for t, t0, m in tiles(n):
                    for c in range(CT):
                        ins = nc.tensor.transpose(bank[:, c * N + t0:c * N + t0 + m],
                                                  zt[0:m, t, c * P:(c + 1) * P], ident[0:m, 0:m])
                ins.then_inc(u_ready.sem, 1)

            def out_half(i, n, half, nxt=None):
                banks = sps if half == 0 else qps
                if half == 0:
                    pe.wait_ge(exp_ok.sem, exp_ok.at(i, 4 if n == N else 2))
                else:
                    pe.wait_ge(pt_lo_ok.sem, pt_lo_ok.at(i, 4))
                for a in range(KT):
                    q = half * KT + a
                    if half == 0 and a % CT == 0:
                        pe.wait_ge(y_lo_ok.sem, y_lo_ok.at(i, a // CT + 1))
                    pe.wait_ge(wo_lo_ok.sem, wo_lo_ok.at(i, q + 1))
                    k, s = K_ORDER[a], q % WST
                    for t, t0, m in tiles(n):
                        ins = three(banks[0:m, t, :], y_hi[:, k, t0:t0 + m], y_lo[:, k, t0:t0 + m],
                                    wo_hi[:, s, :], wo_lo[:, s, :], a == 0, a == KT - 1)
                    ins.then_inc(o_piece.sem, 1)
                    if nxt and a == 3:
                        transposes(i, *nxt)

            def chunk(i, n, nxt):
                def after(name):
                    if type(i) is int and i == 0:
                        j = FIRST.index(name) + 1
                        while FIRST[j] in PREP:
                            weight_sums(PREP.index(FIRST[j]))
                            j += 1

                def prj(name):
                    project(i, n, name)
                    after(name)

                for name in ("b_a", "b_v", "x_q", "c_u"):
                    prj(name)
                scores(i, n, 0)
                prj("a_c")
                probs_t(i, n, 0)
                scores(i, n, 1)
                prj("a_x")
                attend(i, n, 0)
                prj("a_b")
                probs_t(i, n, 1)
                prj("a_g")
                attend(i, n, 1)
                mix(i, n)
                prj("b_g")
                z_rows(i, n)
                prj("c_g")
                prj("x_g")
                z_back(i, n)
                if nxt:
                    transposes(i, *nxt[0])
                out_half(i, n, 0)
                out_half(i, n, 1, nxt[1] if len(nxt) > 1 else None)

            def keys_t(k):
                if k == 0:
                    pe.wait_ge(kv_ok.sem, 2)
                else:
                    pe.wait_ge(kv_in.sem, 64)
                    pe.wait_ge(yx_ok.sem, yx_ok.at(CHUNKS, 0))
                for p in range(PAIRS):
                    for t in range(MT):
                        ins = nc.tensor.transpose(ops[:, p * NMEM + t * P:p * NMEM + (t + 1) * P],
                                                  kv[:, t, p * P:(p + 1) * P], ident[:, :])
                ins.then_inc(ktp.sem, 1)

            def states_out(n):
                for src, ln, b, off in ((glu, HB, 0, 0), (cu, HP, 0, GW), (va, HA, 1, 0)):
                    for c in range(CT):
                        ins = nc.tensor.transpose(sps[0:ln, b, off + c * P:off + (c + 1) * P],
                                                  src[:, c, n:n + ln], ident[:, :])
                ins.then_inc(stp.sem, 1)

            pe.wait_ge(ident_ok.sem, 2)
            pe.wait_ge(c_in.sem, 16 * 9)
            for c in range(CT):
                nc.tensor.transpose(ops[:, c * NR:(c + 1) * NR], z[0:NR, 0, c * P:(c + 1) * P], ident[0:NR, 0:NR])
            nc.tensor.transpose(ops[:, CT * NR:CT * NR + 2 * KT], z[0:2 * KT, 1, 0:P],
                                ident[0:2 * KT, 0:2 * KT]).then_inc(ctr.sem, 1)
            transposes(0, ("m0", "m1"), (0, P))
            transposes(0, ("m2", "m3"), (1, P))
            pe.wait_ge(mn_lo.sem, 4)
            for k in range(KT):
                pe.wait_ge(kw_lo.sem, k + 1)
                for t in range(MT):
                    ins = three(sps[:, t, :], y_hi[:, k, t * P:(t + 1) * P], y_lo[:, k, t * P:(t + 1) * P],
                                wo_hi[:, k % WST, :], wo_lo[:, k % WST, :], k == 0, k == KT - 1)
                ins.then_inc(kvp.sem, 1)
            transposes(0, ("t0", "t1"), (2, P))
            keys_t(0)
            transposes(0, ("t2", "t3"), (3, P))
            for j in range(4):
                weight_sums(j)

            def next_tiles(i, names=("t0", "t1", "t2", "t3")):
                return [(names[0:2], (2 * i + 4, P)), (names[2:4], (2 * i + 5, P))]

            pe.wait_ge(kt_l.sem, 1)
            pe.wait_ge(v_l.sem, 1)
            chunk(0, N, next_tiles(0, ("n0", "n1", "n2", "n3")))
            with pe.Fori(1, LAST) as i:
                chunk(i, N, next_tiles(i))
            chunk(LAST, N, [(("t0", "t1"), (2 * LAST + 4, SAMPLE))])
            keys_t(1)
            pe.wait_ge(r_ok.sem, r_ok.at(LAST, 4))
            states_out(N)
            pe.wait_ge(st_in.sem, 48)
            for c in range(CT):
                nc.tensor.transpose(qps[:, 0, c * P:c * P + HB], z[0:HB, 0, c * P:(c + 1) * P], ident[0:HB, 0:HB])
                nc.tensor.transpose(qps[:, 0, c * P + 32:c * P + 32 + HP], z[0:HP, 1, c * P:(c + 1) * P], ident[0:HP, 0:HP])
                ins = nc.tensor.transpose(qps[:, 0, c * P + 64:c * P + 64 + HA], yc[0:HA, 1, c * P:(c + 1) * P], ident[0:HA, 0:HA])
            ins.then_inc(stp.sem, 1)
            pe.wait_ge(kt_l.sem, 2)
            pe.wait_ge(v_l.sem, 2)
            pe.wait_ge(hist_ok.sem, hist_ok.at(CHUNKS, 3))
            chunk(CHUNKS, SAMPLE, [])
            pe.wait_ge(r_ok.sem, r_ok.at(CHUNKS, 2))
            states_out(SAMPLE)

        @block.scalar
        def _(act):
            def at(i, name):
                n, bank = slot(i, name)
                act.wait_ge(u_ready.sem, n)
                return bank[:, :].rearrange("p (c n) -> p c n", c=CT)

            def scaled_out(i, n, name, dst, func, s):
                u = at(i, name)
                for c in range(CT):
                    f = SPLIT[name] * CT + c
                    ins = nc.scalar.activation(dst[:, c], u[:, c, 0:n], func, scale=inv[:, f:f + 1])
                ins.then_inc(s.sem, 1)

            def squares(j, m, i=0):
                act.wait_ge(x_in.sem, 16 * (j + 1))
                if needed(4 * j):
                    act.wait_ge(x_v.sem, 4 * j)
                if needed(o_sq.at(i, 0)):
                    act.wait_ge(o_sq.sem, o_sq.at(i, 0))
                nc.scalar.activation(junk[0:m, :], xb[0:m, :], ACT.Square,
                                     accum_out=X_SQ[0:m, 0:1]).then_inc(x_sq.sem, 1)

            def rows_hi(i, names, j, t, m):
                for h, name in enumerate(names):
                    n, bank = slot(i, name)
                    act.wait_ge(u_ready.sem, n)
                    src = bank[:, :].rearrange("p (k c) -> p k c", k=4)[:, :, 0:m]
                    nc.scalar.activation(h_hi[:, 4 * h:4 * h + 4, t * P:t * P + m], src, ACT.Copy).then_inc(h_hi_ok.sem, 1)

            def piece_hi(i, q):
                act.wait_ge(raw_in[q % RAW].sem, raw_in[q % RAW].at(i, 16 * (q // RAW + 1)))
                if needed(o_piece.at(i, q - WST + 1)):
                    act.wait_ge(o_piece.sem, o_piece.at(i, q - WST + 1))
                nc.scalar.activation(wo_hi[:, q % WST, :], raw[:, q % RAW, :], ACT.Copy).then_inc(wo_hi_ok.sem, 1)

            def prep(j):
                b, f = j % 2, PREP_FT[j]
                act.wait_ge(wg_ok.sem, j + 1)
                if needed(FIRST.index(f"w{j - 1}") + 1 if j else 0):
                    act.wait_ge(u_ready.sem, FIRST.index(f"w{j - 1}") + 1 if j else 0)
                nc.scalar.activation(mags[:, :, :], stage[:, b], ACT.Abs).then_inc(mags_ok.sem, 1)

            def prep_hi(j):
                b, f = j % 2, PREP_FT[j]
                act.wait_ge(scaled.sem, j + 1)
                nc.scalar.activation(w_hi[:, f], stage[:, b], ACT.Copy).then_inc(whi_ok.sem, 1)

            def exps(i, n, p):
                nt = len(tiles(n))
                for t, t0, m in tiles(n):
                    s = p * nt + t
                    b = s % 2
                    act.wait_ge(nmax_ok.sem, nmax_ok.at(i, p + 1))
                    if s >= 2:
                        act.wait_ge(pt_ready.sem, pt_ready.at(i, (s - 2) // nt + 1))
                    elif type(i) is int and i == 0:
                        act.wait_ge(kv_in.sem, 32)
                        act.wait_ge(v_l.sem, 1)
                    else:
                        act.wait_ge(pt_ready.sem, pt_ready.at(i, 0))
                        if type(i) is int and i == CHUNKS:
                            act.wait_ge(v_l.sem, 2)
                    for h in range(2):
                        ins = nc.scalar.activation(probs[0:m, b, h, :], sps[0:m, h, t * NMEM:(t + 1) * NMEM], ACT.Exp,
                                                   bias=nmax[0:m, s, h:h + 1], scale=1.0,
                                                   accum_out=rsum[0:m, s, h:h + 1])
                    ins.then_inc(exp_ok.sem, 1)

            def probs_hi(i, n, p):
                act.wait_ge(pt_ready.sem, pt_ready.at(i, p + 1))
                if needed(pv_ready.at(i, p)):
                    act.wait_ge(pv_ready.sem, pv_ready.at(i, p))
                for h in range(2):
                    src = qps[:, h, :].rearrange("p (k n) -> p k n", k=MT)[:, :, 0:n]
                    nc.scalar.activation(pt_hi[:, h, :, 0:n], src, ACT.Copy).then_inc(pt_hi_ok.sem, 1)

            def y_high(i, n, k, src, s):
                act.wait_ge(s.sem, s.at(i, 1))
                nc.scalar.activation(y_hi[:, k:k + CT, 0:n], src, ACT.Copy).then_inc(y_hi_ok.sem, 1)

            def chunk(i, n, nxt):
                first = type(i) is int and i == 0

                def prepare(g):
                    if first:
                        for j in (2 * g + 4, 2 * g + 5):
                            prep(j)
                        for j in (2 * g + 4, 2 * g + 5):
                            prep_hi(j)

                if needed(y_lo_ok.at(i, 0)):
                    act.wait_ge(y_lo_ok.sem, y_lo_ok.at(i, 0))
                scaled_out(i, n, "b_a", gate[:, 0, :, 0:n], ACT.Sigmoid, sig_ok)
                prepare(0)
                if nxt:
                    squares(nxt[0][1], nxt[0][3], i)
                prepare(1)
                scaled_out(i, n, "x_q", dq_hi[:, :, 0:n], ACT.Copy, q_hi)
                prepare(2)
                act.wait_ge(hist_ok.sem, hist_ok.at(i, 3))
                if needed(d_ok.at(i, 0)):
                    act.wait_ge(d_ok.sem, d_ok.at(i, 0))
                scaled_out(i, n, "c_u", cu[:, :, HP:HP + n], ACT.Copy, cu_ok)
                prepare(3)
                exps(i, n, 0)
                scaled_out(i, n, "a_c", gate[:, 1, :, 0:n], ACT.Copy, ac_ok)
                prepare(4)
                probs_hi(i, n, 0)
                exps(i, n, 1)
                prepare(5)
                act.wait_ge(d_ok.sem, d_ok.at(i, 1))
                act.wait_ge(s_ready.sem, s_ready.at(i, 2))
                nc.scalar.activation(dq_hi[:, :, 0:n], yc[:, :, 0:n], ACT.Copy).then_inc(d_hi.sem, 1)
                prepare(6)
                probs_hi(i, n, 1)
                scaled_out(i, n, "a_g", gate[:, 2, :, 0:n], ACT.Silu, ag_ok)
                prepare(7)
                act.wait_ge(d_lo.sem, d_lo.at(i, 1))
                u = at(i, "mix")
                for c in range(CT):
                    ins = nc.scalar.activation(yc[:, c, 0:n], u[:, c, 0:n], ACT.Identity,
                                               scale=cst[:, c, R_PS:R_PS + 1], bias=pbs[:, c:c + 1])
                ins.then_inc(mix_ok.sem, 1)
                act.wait_ge(glu_ok.sem, glu_ok.at(i, 1))
                scaled_out(i, n, "b_g", gate[:, 0, :, 0:n], ACT.Silu, bg_ok)
                prepare(8)
                y_high(i, n, 0, ya[:, :, 0:n], ya_ok)
                act.wait_ge(va_ok.sem, va_ok.at(i, 1))
                scaled_out(i, n, "c_g", gate[:, 1, :, 0:n], ACT.Silu, cg_ok)
                for q in range(WST):
                    piece_hi(i, q)
                scaled_out(i, n, "x_g", gate[:, 2, :, 0:n], ACT.Silu, xg_ok)
                y_high(i, n, 4, yc[:, :, 0:n], yc_ok)
                y_high(i, n, 6, gate[:, 2, :, 0:n], yx_ok)
                u = at(i, "zb")
                for c in range(CT):
                    ins = nc.scalar.activation(z[:, c, 0:n], u[:, c, 0:n], ACT.Silu,
                                               scale=cst[:, c, R_LNG:R_LNG + 1], bias=cst[:, c, R_LNB:R_LNB + 1])
                ins.then_inc(zs_ok.sem, 1)
                if nxt:
                    rows_hi(i, nxt[0][0], *nxt[0][1:])
                y_high(i, n, 2, z[:, :, 0:n], yb_ok)
                for q in range(WST, PIECES):
                    piece_hi(i, q)
                    if q == KT + 1 and len(nxt) > 1:
                        squares(nxt[1][1], nxt[1][3], i)
                    if q == KT + 6 and len(nxt) > 1:
                        rows_hi(i, nxt[1][0], *nxt[1][1:])
                nt = len(tiles(n))
                act.wait_ge(r_ok.sem, r_ok.at(i, 2 * nt))
                if needed(o_v.at(i, 0)):
                    act.wait_ge(o_v.sem, o_v.at(i, 0))
                for t, _, m in tiles(n):
                    if needed(o_sq.at(i, t)):
                        act.wait_ge(o_sq.sem, o_sq.at(i, t))
                    if nxt:
                        act.wait_ge(x_sq.sem, nxt[-1][1] + 1)
                    nc.scalar.activation(junk[0:m, :], ob[0:m, t, :], ACT.Square,
                                         accum_out=O_SQ[0:m, t:t + 1]).then_inc(o_sq.sem, 1)
                act.wait_ge(o_newton.sem, o_newton.at(i, 4 * NEWTON))
                for t, _, m in tiles(n):
                    ins = nc.scalar.activation(ob[0:m, t, :], ob[0:m, t, :], ACT.Copy, scale=O_Y[0:m, t:t + 1])
                ins.then_inc(o_rs.sem, 1)

            def keys_values_hi(k):
                act.wait_ge(ktp.sem, k + 1)
                if k == 0:
                    act.wait_ge(zero_ok.sem, 3)
                nc.scalar.activation(kt_hi[:, :, :], ops[:, :].rearrange("p (a m) -> p a m", a=PAIRS), ACT.Copy,
                                     scale=HD ** -0.5).then_inc(kt_h.sem, 1)
                for t in range(MT):
                    src = kv[:, t, GW:2 * GW].rearrange("p (a h d) -> p a h d", a=PAIRS, h=2)
                    dst = v_hi[:, t].rearrange("p a (s d) -> p a s d", s=3)[:, :, 0::2, :]
                    ins = nc.scalar.activation(dst, src, ACT.Copy)
                ins.then_inc(v_h.sem, 1)

            def states_ok(k):
                act.wait_ge(stp.sem, 2 * k + 1)
                nc.scalar.activation(ya[0:HB, 0, :], sps[0:HB, 0, 0:GW], ACT.Copy)
                nc.scalar.activation(ya[0:HP, 1, :], sps[0:HP, 0, GW:2 * GW], ACT.Copy).then_inc(st_ok.sem, 1)
                nc.scalar.activation(yc[0:HA, 0, :], sps[0:HA, 1, 0:GW], ACT.Copy).then_inc(st_ok.sem, 1)

            act.wait_ge(ctr.sem, 1)
            nc.scalar.activation(cst[:, :, :], ops[:, 0:CT * NR].rearrange("p (c r) -> p c r", c=CT), ACT.Copy)
            nc.scalar.activation(gcol[:, :], ops[:, CT * NR:CT * NR + 2 * KT], ACT.Copy).then_inc(cev.sem, 1)
            squares(0, P)
            act.wait_ge(cev.sem, 1)

            def memory_hi(t):
                for h in range(2):
                    name = f"m{2 * t + h}"
                    n, bank = slot(0, name)
                    act.wait_ge(u_ready.sem, n)
                    for k in range(4):
                        kk = 4 * h + k
                        ins = nc.scalar.activation(y_hi[:, kk, t * P:(t + 1) * P], bank[:, k * P:(k + 1) * P], ACT.Copy,
                                                   scale=gcol[:, KT + kk:KT + kk + 1])
                    ins.then_inc(mn_hi.sem, 1)

            def kw(k):
                b = k % 4
                act.wait_ge(kw_in[b].sem, 32 * (k // 4 + 1))
                if needed(k - WST + 1):
                    act.wait_ge(kvp.sem, k - WST + 1)
                nc.scalar.activation(wo_hi[:, k % WST, :], ob[:, b // 2, (b % 2) * HALF:(b % 2 + 1) * HALF],
                                     ACT.Copy).then_inc(kw_hi.sem, 1)

            memory_hi(0)
            squares(1, P)
            for k in range(4):
                kw(k)
            memory_hi(1)
            squares(2, P)
            for k in range(4, KT):
                kw(k)
            act.wait_ge(kvp.sem, KT)
            nc.scalar.activation(kv[:, :, :], sps[:, :, :], ACT.Copy).then_inc(kv_ok.sem, 2)
            rows_hi(0, ("t0", "t1"), 2, 0, P)
            act.wait_ge(kv_ok.sem, 2)
            keys_values_hi(0)
            squares(3, P)
            rows_hi(0, ("t2", "t3"), 3, 1, P)
            for j in (0, 2):
                prep(j)
                prep(j + 1)
                prep_hi(j)
                prep_hi(j + 1)
            act.wait_ge(pw_in.sem, 64)
            nc.scalar.activation(pw_hi[:, :, :], ya[:, 0, :].rearrange("p (c m) -> p c m", c=CT), ACT.Copy).then_inc(pw_ok.sem, 1)

            def next_tiles(i, names=("t0", "t1", "t2", "t3")):
                return [(names[0:2], 2 * i + 4, 0, P), (names[2:4], 2 * i + 5, 1, P)]

            chunk(0, N, next_tiles(0, ("n0", "n1", "n2", "n3")))
            with act.Fori(1, LAST) as i:
                chunk(i, N, next_tiles(i))
            chunk(LAST, N, [(("t0", "t1"), 2 * LAST + 4, 0, SAMPLE)])
            keys_values_hi(1)
            states_ok(0)
            chunk(CHUNKS, SAMPLE, [])
            states_ok(1)

        @block.vector
        def _(dve):
            def at(i, name):
                n, bank = slot(i, name)
                dve.wait_ge(u_ready.sem, n)
                return bank[:, :].rearrange("p (c n) -> p c n", c=CT)

            def rsqrt_seed(s, i, k, sq, v, sh, y, mul, add=EPS):
                if needed(s.at(i, k)):
                    dve.wait_ge(s.sem, s.at(i, k))
                nc.vector.tensor_scalar(sh, sq, mul, add, ALU.mult, ALU.add).then_inc(s.sem, 1)
                nc.vector.tensor_scalar(v, sq, -0.5 * mul, -0.5 * add, ALU.mult, ALU.add).then_inc(s.sem, 1)
                dve.wait_ge(s.sem, s.at(i, k + 1))
                nc.vector.tensor_scalar(y.bitcast(I32), sh.bitcast(I32), 1, None, ALU.logical_shift_right).then_inc(s.sem, 1)
                dve.wait_ge(s.sem, s.at(i, k + 3))
                nc.vector.tensor_scalar(y.bitcast(I32), y.bitcast(I32), -1.0, float(MAGIC), ALU.mult, ALU.add).then_inc(s.sem, 1)

            def rows_seed(j, m):
                dve.wait_ge(x_sq.sem, j + 1)
                if needed(j):
                    dve.wait_ge(x_scaled.sem, j)
                rsqrt_seed(x_v, 0, 4 * j, X_SQ[0:m, 0:1], X_V[0:m, 0:1], X_SH[0:m, 0:1], X_Y[0:m, 0:1], 1.0 / D)

            def rows_scale(j, m, factor):
                dve.wait_ge(x_newton.sem, 4 * NEWTON * (j + 1))
                nc.vector.tensor_scalar(xb[0:m, :], xb[0:m, :], X_Y[0:m, 0:1], factor, ALU.mult, ALU.mult).then_inc(x_scaled.sem, 1)

            def rows_lo(i, names, hi_base, t, m):
                for h, name in enumerate(names):
                    n, bank = slot(i, name)
                    dve.wait_ge(h_hi_ok.sem, hi_base + h + 1)
                    src = bank[:, :].rearrange("p (k c) -> p k c", k=4)[:, :, 0:m]
                    o = (slice(None), slice(4 * h, 4 * h + 4), slice(t * P, t * P + m))
                    nc.vector.tensor_tensor(h_lo[o], src, h_hi[o], ALU.subtract).then_inc(h_lo_ok.sem, 1)

            def piece_lo(i, q):
                dve.wait_ge(wo_hi_ok.sem, wo_hi_ok.at(i, q + 1))
                nc.vector.tensor_tensor(wo_lo[:, q % WST, :], raw[:, q % RAW, :],
                                        wo_hi[:, q % WST, :].bitcast(F32), ALU.subtract).then_inc(wo_lo_ok.sem, 1)

            def prep_sums(j):
                n, bank = slot(0, f"w{j}")
                f = PREP_FT[j]
                dve.wait_ge(u_ready.sem, n)
                if needed(5 * j):
                    dve.wait_ge(l1_s.sem, 5 * j)
                if needed(j):
                    dve.wait_ge(scaled.sem, j)
                nc.vector.tensor_scalar(l1[:, 0, :], bank[:, 0:P], 2.0 ** -100, None, ALU.max).then_inc(l1_s.sem, 1)
                dve.wait_ge(l1_s.sem, 5 * j + 1)
                nc.vector.tensor_scalar(l1[:, 1, :].bitcast(I32), l1[:, 0, :].bitcast(I32), 0x7F800000, None,
                                        ALU.bitwise_and).then_inc(l1_s.sem, 1)
                dve.wait_ge(l1_s.sem, 5 * j + 2)
                nc.vector.tensor_scalar(l1[:, 2, :].bitcast(I32), l1[:, 1, :].bitcast(I32), -1.0,
                                        float((WEXP + 254) << 23), ALU.mult, ALU.add).then_inc(l1_s.sem, 1)
                nc.vector.scalar_tensor_tensor(l1[:, 0, :], l1[:, 1, :], 2.0 ** -WEXP / XSCALE, ident[:, :],
                                               ALU.mult, ALU.mult).then_inc(l1_s.sem, 1)
                dve.wait_ge(l1_s.sem, 5 * j + 4)
                nc.vector.reduce_sum(inv[:, f:f + 1], l1[:, 0, :], axis=AX.X).then_inc(l1_s.sem, 1)

            def prep_scale(j):
                b = j % 2
                nc.vector.tensor_tensor(stage[:, b], stage[:, b],
                                        l1[:, 2, :].unsqueeze(1).to_broadcast([P, KT, P]), ALU.mult).then_inc(scaled.sem, 1)

            def prep_lo(j):
                b, f = j % 2, PREP_FT[j]
                dve.wait_ge(whi_ok.sem, j + 1)
                nc.vector.tensor_tensor(w_lo[:, f], stage[:, b], w_hi[:, f], ALU.subtract).then_inc(wlo_ok.sem, 1)

            def prep(j):
                prep_sums(j)
                prep_scale(j)
                prep_lo(j)

            def taps(i, n, k0, k1):
                for k in range(k0, k1):
                    for c in range(CT):
                        w = cst[:, c, R_BW + k:R_BW + k + 1]
                        if k == 0:
                            ins = nc.vector.tensor_scalar(z[:, c, 0:n], glu[:, c, k:k + n], w,
                                                          cst[:, c, R_BIAS:R_BIAS + 1], ALU.mult, ALU.add)
                        else:
                            dve.wait_ge(conv_step.sem, conv_step.at(i, 2 * (k - 1) + c + 1))
                            ins = nc.vector.scalar_tensor_tensor(z[:, c, 0:n], glu[:, c, k:k + n], w, z[:, c, 0:n],
                                                                 ALU.mult, ALU.add)
                        ins.then_inc(conv_step.sem, 1)

            def softmax_max(i, n, p):
                nt = len(tiles(n))
                m = min(n, P)
                dve.wait_ge(s_ready.sem, s_ready.at(i, p + 1))
                nc.vector.reduce_max(nmax[0:m, p * nt:(p + 1) * nt, :].rearrange("p t h -> p h t"),
                                     sps[0:m, :, 0:nt * NMEM].rearrange("p h (t k) -> p h t k", k=NMEM),
                                     axis=AX.X, negate=True).then_inc(nmax_ok.sem, 1)

            def softmax_norm(i, n, p):
                nt = len(tiles(n))
                for t, t0, m in tiles(n):
                    s = p * nt + t
                    dve.wait_ge(exp_ok.sem, exp_ok.at(i, s + 1))
                    nc.vector.reciprocal(rcp[0:m, s, :], rsum[0:m, s, :]).then_inc(rcp_ok.sem, 1)
                for t, t0, m in tiles(n):
                    s = p * nt + t
                    dve.wait_ge(rcp_ok.sem, rcp_ok.at(i, s + 1))
                    for h in range(2):
                        ins = nc.vector.tensor_scalar(probs[0:m, s % 2, h, :], probs[0:m, s % 2, h, :],
                                                      rcp[0:m, s, h:h + 1], None, ALU.mult)
                    ins.then_inc(p_ok.sem, 1)

            def probs_lo(i, n, p):
                for h in range(2):
                    dve.wait_ge(pt_hi_ok.sem, pt_hi_ok.at(i, 2 * p + h + 1))
                    src = qps[:, h, :].rearrange("p (k n) -> p k n", k=MT)[:, :, 0:n]
                    nc.vector.tensor_tensor(pt_lo[:, h, :, 0:n], src, pt_hi[:, h, :, 0:n].bitcast(F32), ALU.subtract).then_inc(pt_lo_ok.sem, 1)

            def chunk(i, n, nxt):
                first = type(i) is int and i == 0
                nt = len(tiles(n))

                def prepare(g):
                    if first:
                        for j in (2 * g + 4, 2 * g + 5):
                            prep(j)

                if not first and not (type(i) is int and i == CHUNKS):
                    dve.wait_ge(win_ok.sem, win_ok.at(i, 0))
                    nc.vector.tensor_copy(glu[:, :, 0:HB], glu[:, :, N:N + HB]).then_inc(hist_ok.sem, 1)
                    nc.vector.tensor_copy(va[:, :, 0:HA], va[:, :, N:N + HA]).then_inc(hist_ok.sem, 1)
                    nc.vector.tensor_copy(cu[:, :, 0:HP], cu[:, :, N:N + HP]).then_inc(hist_ok.sem, 1)
                    dve.wait_ge(hist_ok.sem, hist_ok.at(i, 3))
                prepare(0)
                dve.wait_ge(sig_ok.sem, sig_ok.at(i, 1))
                u = at(i, "b_v")
                for c in range(CT):
                    f = SPLIT["b_v"] * CT + c
                    ins = nc.vector.scalar_tensor_tensor(glu[:, c, HB:HB + n], u[:, c, 0:n], inv[:, f:f + 1],
                                                         gate[:, 0, c, 0:n], ALU.mult, ALU.mult)
                ins.then_inc(glu_ok.sem, 1)
                prepare(1)
                dve.wait_ge(glu_ok.sem, glu_ok.at(i, 1))
                if needed(y_lo_ok.at(i, 0)):
                    dve.wait_ge(y_lo_ok.sem, y_lo_ok.at(i, 0))
                if nxt:
                    rows_seed(nxt[0][0], nxt[0][2])
                taps(i, n, 0, 6)
                dve.wait_ge(q_hi.sem, q_hi.at(i, 1))
                u = at(i, "x_q")
                for c in range(CT):
                    f = SPLIT["x_q"] * CT + c
                    ins = nc.vector.scalar_tensor_tensor(dq_lo[:, c, 0:n], u[:, c, 0:n], inv[:, f:f + 1],
                                                         dq_hi[:, c, 0:n].bitcast(F32), ALU.mult, ALU.subtract)
                ins.then_inc(q_lo.sem, 1)
                prepare(2)
                prepare(3)
                taps(i, n, 6, 11)
                softmax_max(i, n, 0)
                if nxt:
                    rows_scale(nxt[0][0], nxt[0][2], XSCALE)
                taps(i, n, 11, 14)
                softmax_norm(i, n, 0)
                prepare(4)
                taps(i, n, 14, 18)
                probs_lo(i, n, 0)
                softmax_max(i, n, 1)
                taps(i, n, 18, 20)
                softmax_norm(i, n, 1)
                dve.wait_ge(win_ok.sem, win_ok.at(i, 4))
                if needed(yc_ok.at(i, 0)):
                    dve.wait_ge(yc_ok.sem, yc_ok.at(i, 0))
                for c in range(CT):
                    for h in range(2):
                        r = slice(h * HD, (h + 1) * HD)
                        sums = (sa[r, c, S2:S2 + n], sb_[r, c, S4:S4 + n])[h]
                        ins = nc.vector.scalar_tensor_tensor(yc[r, c, 0:n], sums, 1.0 / WINDOWS[2 * c + h],
                                                             cu[r, c, HP:HP + n], ALU.mult, ALU.subtract)
                ins.then_inc(d_ok.sem, 1)
                dve.wait_ge(ac_ok.sem, ac_ok.at(i, 1))
                u = at(i, "a_x")
                for c in range(CT):
                    f = SPLIT["a_x"] * CT + c
                    ins = nc.vector.scalar_tensor_tensor(va[:, c, HA:HA + n], u[:, c, 0:n], inv[:, f:f + 1],
                                                         gate[:, 1, c, 0:n], ALU.mult, ALU.mult)
                ins.then_inc(va_ok.sem, 1)
                prepare(5)
                taps(i, n, 20, 22)
                dve.wait_ge(d_hi.sem, d_hi.at(i, 1))
                nc.vector.tensor_tensor(dq_lo[:, :, 0:n], yc[:, :, 0:n], dq_hi[:, :, 0:n].bitcast(F32), ALU.subtract).then_inc(d_lo.sem, 1)
                dve.wait_ge(va_ok.sem, va_ok.at(i, 1))
                if needed(y_lo_ok.at(i, 0)):
                    dve.wait_ge(y_lo_ok.sem, y_lo_ok.at(i, 0))
                if first:
                    dve.wait_ge(pw_ok.sem, 2)
                for k in range(TA):
                    for c in range(CT):
                        w = cst[:, c, R_AW + k:R_AW + k + 1]
                        if k == 0:
                            ins = nc.vector.tensor_scalar(ya[:, c, 0:n], va[:, c, k:k + n], w, None, ALU.mult)
                        else:
                            dve.wait_ge(conv_a.sem, conv_a.at(i, 2 * (k - 1) + c + 1))
                            ins = nc.vector.scalar_tensor_tensor(ya[:, c, 0:n], va[:, c, k:k + n], w, ya[:, c, 0:n],
                                                                 ALU.mult, ALU.add)
                        ins.then_inc(conv_a.sem, 1)
                taps(i, n, 22, 26)
                u = at(i, "a_b")
                for c in range(CT):
                    f = SPLIT["a_b"] * CT + c
                    dve.wait_ge(conv_a.sem, conv_a.at(i, 2 * (TA - 1) + c + 1))
                    nc.vector.scalar_tensor_tensor(ya[:, c, 0:n], u[:, c, 0:n], inv[:, f:f + 1],
                                                   ya[:, c, 0:n], ALU.mult, ALU.mult).then_inc(conv_a.sem, 1)
                prepare(6)
                probs_lo(i, n, 1)
                taps(i, n, 26, TB)
                prepare(7)
                prepare(8)
                if needed(zt_ok.at(i, 0)):
                    dve.wait_ge(zt_ok.sem, zt_ok.at(i, 0))
                n_zf, bank = slot(i, "zf")
                dve.wait_ge(u_ready.sem, n_zf)
                for t, _, m in tiles(n):
                    ins = nc.vector.bn_stats(bn6[0:m, t, :], bank[0:m, t * GW:(t + 1) * GW])
                ins.then_inc(bn_s.sem, 1)
                dve.wait_ge(bn_s.sem, bn_s.at(i, 1))
                dve.wait_ge(ag_ok.sem, ag_ok.at(i, 1))
                dve.wait_ge(conv_a.sem, conv_a.at(i, 4 * CT))
                nc.vector.tensor_tensor(ya[:, :, 0:n], ya[:, :, 0:n], gate[:, 2, :, 0:n], ALU.mult).then_inc(ya_ok.sem, 1)
                for t, _, m in tiles(n):
                    ins = nc.vector.bn_aggr(mv[0:m, t, :], bn6[0:m, t, :])
                ins.then_inc(bn_s.sem, 1)
                dve.wait_ge(bn_s.sem, bn_s.at(i, 2))
                m0 = min(n, P)
                rsqrt_seed(ln_v, i, 0, mv[0:m0, 0:nt, 1], L_V[0:m0, 0:nt], L_SH[0:m0, 0:nt], L_Y[0:m0, 0:nt], 1.0)
                for q in range(WST):
                    piece_lo(i, q)
                dve.wait_ge(ln_newton.sem, ln_newton.at(i, 4 * NEWTON))
                for t, _, m in tiles(n):
                    ins = nc.vector.tensor_scalar(zt[0:m, t, :], bank[0:m, t * GW:(t + 1) * GW], mv[0:m, t, 0:1],
                                                  L_Y[0:m, t:t + 1], ALU.subtract, ALU.mult)
                ins.then_inc(zt_ok.sem, 1)
                dve.wait_ge(xg_ok.sem, xg_ok.at(i, 1))
                dve.wait_ge(pv_ready.sem, pv_ready.at(i, 2))
                nc.vector.tensor_tensor(gate[:, 2, :, 0:n], ops[:, :].rearrange("p (c n) -> p c n", c=CT)[:, :, 0:n],
                                        gate[:, 2, :, 0:n], ALU.mult).then_inc(yx_ok.sem, 1)
                dve.wait_ge(zs_ok.sem, zs_ok.at(i, 1))
                dve.wait_ge(bg_ok.sem, bg_ok.at(i, 1))
                nc.vector.tensor_tensor(z[:, :, 0:n], z[:, :, 0:n], gate[:, 0, :, 0:n], ALU.mult).then_inc(yb_ok.sem, 1)
                if nxt:
                    rows_lo(i, nxt[0][4], nxt[0][1], 0, nxt[0][2])
                for q in range(WST, PIECES):
                    piece_lo(i, q)
                    if q == KT + 2 and len(nxt) > 1:
                        rows_seed(nxt[1][0], nxt[1][2])
                    if q == KT + 4 and len(nxt) > 1:
                        rows_scale(nxt[1][0], nxt[1][2], XSCALE)
                    if q == KT + 2:
                        add_half(i, n, 0)
                    if q == KT + 6 and len(nxt) > 1:
                        rows_lo(i, nxt[1][4], nxt[1][1], 1, nxt[1][2])
                add_half(i, n, 1)
                dve.wait_ge(o_sq.sem, o_sq.at(i, nt))
                if needed(o_rs.at(i, 0)):
                    dve.wait_ge(o_rs.sem, o_rs.at(i, 0))
                rsqrt_seed(o_v, i, 0, O_SQ[0:m0, 0:nt], O_V[0:m0, 0:nt], O_SH[0:m0, 0:nt], O_Y[0:m0, 0:nt], 1.0 / D)

            def add_half(i, n, half):
                banks = sps if half == 0 else qps
                dve.wait_ge(o_piece.sem, o_piece.at(i, (half + 1) * KT))
                for t, _, m in tiles(n):
                    if half == 0:
                        dve.wait_ge(res_in[t].sem, res_in[t].at(i, 16))
                    c = slice(half * HALF, (half + 1) * HALF)
                    nc.vector.tensor_tensor(ob[0:m, t, c], banks[0:m, t, :], ob[0:m, t, c], ALU.add).then_inc(r_ok.sem, 1)

            def keys_values_lo(k):
                dve.wait_ge(kt_h.sem, k + 1)
                nc.vector.scalar_tensor_tensor(kt_lo[:, :, :], ops[:, :].rearrange("p (a m) -> p a m", a=PAIRS),
                                               HD ** -0.5, kt_hi[:, :, :].bitcast(F32), ALU.mult, ALU.subtract).then_inc(kt_l.sem, 1)
                dve.wait_ge(v_h.sem, k + 1)
                for t in range(MT):
                    src = kv[:, t, GW:2 * GW].rearrange("p (a h d) -> p a h d", a=PAIRS, h=2)
                    hi = v_hi[:, t].rearrange("p a (s d) -> p a s d", s=3)[:, :, 0::2, :]
                    lo = v_lo[:, t].rearrange("p a (s d) -> p a s d", s=3)[:, :, 0::2, :]
                    ins = nc.vector.tensor_tensor(lo, src, hi.bitcast(F32), ALU.subtract)
                ins.then_inc(v_l.sem, 1)

            nc.vector.memset(ya[:, 0, :], 0.0).then_inc(zero_ok.sem, 1)
            for buf in (glu[:, :, 0:HB], va[:, :, 0:HA], cu[:, :, 0:HP]):
                nc.vector.memset(buf, 0.0).then_inc(hist_ok.sem, 1)
            for buf in (v_hi, v_lo):
                nc.vector.memset(buf[:, :, :, HD:2 * HD].bitcast(F32), 0.0).then_inc(zero_ok.sem, 1)
            nc.vector.memset(c15[:, :], 1.5).then_inc(zero_ok.sem, 1)
            dve.wait_ge(ramp_s.sem, 2)
            for c in range(CT):
                for h in range(2):
                    r = slice(h * HD, (h + 1) * HD)
                    ins = nc.vector.tensor_scalar(ramp[r, c, :], ramp[r, c, :], float(WINDOWS[2 * c + h]),
                                                  1.0 / WINDOWS[2 * c + h], ALU.min, ALU.mult)
            ins.then_inc(ramp_s.sem, 1)
            dve.wait_ge(ramp_s.sem, 3)
            nc.vector.reciprocal(ramp[:, :, :], ramp[:, :, :]).then_inc(ramp_s.sem, 1)
            dve.wait_ge(cev.sem, 1)
            nc.vector.tensor_tensor(pbs[:, :], cst[:, :, R_PB], cst[:, :, R_PS], ALU.mult).then_inc(consts_ok.sem, 1)
            rows_seed(0, P)
            rows_scale(0, P, 1.0)

            def memory_lo(t):
                for h in range(2):
                    dve.wait_ge(mn_hi.sem, 2 * t + h + 1)
                    _, bank = slot(0, f"m{2 * t + h}")
                    for k in range(4):
                        kk = 4 * h + k
                        ins = nc.vector.scalar_tensor_tensor(y_lo[:, kk, t * P:(t + 1) * P], bank[:, k * P:(k + 1) * P],
                                                             gcol[:, KT + kk:KT + kk + 1],
                                                             y_hi[:, kk, t * P:(t + 1) * P].bitcast(F32), ALU.mult, ALU.subtract)
                    ins.then_inc(mn_lo.sem, 1)

            def kw(k):
                b = k % 4
                dve.wait_ge(kw_hi.sem, k + 1)
                nc.vector.tensor_tensor(wo_lo[:, k % WST, :], ob[:, b // 2, (b % 2) * HALF:(b % 2 + 1) * HALF],
                                        wo_hi[:, k % WST, :].bitcast(F32), ALU.subtract).then_inc(kw_lo.sem, 1)

            memory_lo(0)
            rows_seed(1, P)
            rows_scale(1, P, 1.0)
            for k in range(4):
                kw(k)
            memory_lo(1)
            rows_seed(2, P)
            rows_scale(2, P, XSCALE)
            for k in range(4, KT):
                kw(k)
            rows_lo(0, ("t0", "t1"), 0, 0, P)
            keys_values_lo(0)
            rows_seed(3, P)
            rows_scale(3, P, XSCALE)
            rows_lo(0, ("t2", "t3"), 2, 1, P)
            for j in range(4):
                prep(j)
            dve.wait_ge(pw_ok.sem, 1)
            nc.vector.tensor_tensor(pw_lo[:, :, :], ya[:, 0, :].rearrange("p (c m) -> p c m", c=CT),
                                    pw_hi[:, :, :].bitcast(F32), ALU.subtract).then_inc(pw_ok.sem, 1)

            def next_tiles(i, names=("t0", "t1", "t2", "t3")):
                return [(2 * i + 4, 4 * i + 4, P, 0, names[0:2]), (2 * i + 5, 4 * i + 6, P, 1, names[2:4])]

            chunk(0, N, next_tiles(0, ("n0", "n1", "n2", "n3")))
            with dve.Fori(1, LAST) as i:
                chunk(i, N, next_tiles(i))
            chunk(LAST, N, [(2 * LAST + 4, 4 * LAST + 4, SAMPLE, 0, ("t0", "t1"))])
            keys_values_lo(1)
            dve.wait_ge(stp.sem, 2)
            for c in range(CT):
                nc.vector.tensor_copy(glu[:, c, 0:HB], qps[:, 0, c * P:c * P + HB])
                nc.vector.tensor_copy(cu[:, c, 0:HP], qps[:, 0, c * P + 32:c * P + 32 + HP])
                ins = nc.vector.tensor_copy(va[:, c, 0:HA], qps[:, 0, c * P + 64:c * P + 64 + HA])
            ins.then_inc(hist_ok.sem, 3)
            dve.wait_ge(hist_ok.sem, hist_ok.at(CHUNKS, 3))
            dve.wait_ge(stored_st.sem, 48)
            chunk(CHUNKS, SAMPLE, [])

        @block.gpsimd
        def _(pool):
            def newton(s, i, k, v, y, tmp):
                for r in range(NEWTON):
                    b = k + 4 * r
                    if needed(s.at(i, b)):
                        pool.wait_ge(s.sem, s.at(i, b))
                    nc.gpsimd.tensor_tensor(tmp, y, y, ALU.mult).then_inc(s.sem, 1)
                    pool.wait_ge(s.sem, s.at(i, b + 1))
                    nc.gpsimd.tensor_tensor(tmp, tmp, v, ALU.mult).then_inc(s.sem, 1)
                    pool.wait_ge(s.sem, s.at(i, b + 2))
                    nc.gpsimd.tensor_tensor(tmp, tmp, c15[0:tmp.shape[0], 0:tmp.shape[1]], ALU.add).then_inc(s.sem, 1)
                    pool.wait_ge(s.sem, s.at(i, b + 3))
                    nc.gpsimd.tensor_tensor(y, y, tmp, ALU.mult).then_inc(s.sem, 1)

            def rows_newton(j, m):
                pool.wait_ge(x_v.sem, 4 * j + 4)
                newton(x_newton, 0, 4 * NEWTON * j, X_V[0:m, 0:1], X_Y[0:m, 0:1], X_T[0:m, 0:1])

            def prep(j):
                b = j % 2
                pool.wait_ge(stage_in[b].sem, 16 * (j // 2 + 1))
                nc.gpsimd.tensor_tensor(stage[:, b], stage[:, b], gcol[:, 0:KT].unsqueeze(2).to_broadcast([P, KT, P]),
                                        ALU.mult).then_inc(wg_ok.sem, 1)

            def y_low(i, n, k, src, a):
                pool.wait_ge(y_hi_ok.sem, y_hi_ok.at(i, a + 1))
                nc.gpsimd.tensor_tensor(y_lo[:, k:k + CT, 0:n], src, y_hi[:, k:k + CT, 0:n].bitcast(F32),
                                        ALU.subtract).then_inc(y_lo_ok.sem, 1)

            def chunk(i, n, nxt):
                first = type(i) is int and i == 0
                nt = len(tiles(n))

                def prepare(g):
                    if first:
                        for j in (2 * g + 4, 2 * g + 5):
                            prep(j)

                prepare(0)
                prepare(1)
                if nxt:
                    rows_newton(nxt[0][0], nxt[0][1])
                prepare(2)
                pool.wait_ge(cu_ok.sem, cu_ok.at(i, 1))
                if needed(zs_ok.at(i, 0)):
                    pool.wait_ge(zs_ok.sem, zs_ok.at(i, 0))
                nc.gpsimd.tensor_tensor(sa[:, :, 0:S2 + n], cu[:, :, 1:HP + n], cu[:, :, 0:HP + n - 1], ALU.add).then_inc(win_ok.sem, 1)
                pool.wait_ge(win_ok.sem, win_ok.at(i, 1))
                nc.gpsimd.tensor_tensor(sb_[:, :, 0:S4 + n], sa[:, :, 2:S2 + n], sa[:, :, 0:S2 + n - 2], ALU.add).then_inc(win_ok.sem, 1)
                pool.wait_ge(win_ok.sem, win_ok.at(i, 2))
                nc.gpsimd.tensor_tensor(sa[:, 1, 6:S2 + n], sb_[:, 1, 4:S4 + n], sb_[:, 1, 0:S4 + n - 4], ALU.add).then_inc(win_ok.sem, 1)
                pool.wait_ge(win_ok.sem, win_ok.at(i, 3))
                r = slice(HD, P)
                last = nc.gpsimd.tensor_tensor(sb_[r, 1, S4:S4 + n], sa[r, 1, S2:S2 + n], sa[r, 1, S2 - 8:S2 + n - 8], ALU.add)
                if first:
                    last.then_inc(ramp_s.sem, 1)
                    pool.wait_ge(ramp_s.sem, 5)
                    nc.gpsimd.tensor_tensor(sa[0:HD, :, S2:S2 + 16], sa[0:HD, :, S2:S2 + 16], ramp[0:HD], ALU.mult)
                    last = nc.gpsimd.tensor_tensor(sb_[r, :, S4:S4 + 16], sb_[r, :, S4:S4 + 16], ramp[r], ALU.mult)
                last.then_inc(win_ok.sem, 1)
                pool.wait_ge(win_ok.sem, win_ok.at(i, 4))
                for g in range(3, 8):
                    prepare(g)
                prepare(8)
                y_low(i, n, 0, ya[:, :, 0:n], 0)
                pool.wait_ge(ln_v.sem, ln_v.at(i, 4))
                m0 = min(n, P)
                newton(ln_newton, i, 0, L_V[0:m0, 0:nt], L_Y[0:m0, 0:nt], L_T[0:m0, 0:nt])
                pool.wait_ge(cg_ok.sem, cg_ok.at(i, 1))
                pool.wait_ge(mix_ok.sem, mix_ok.at(i, 1))
                nc.gpsimd.tensor_tensor(yc[:, :, 0:n], yc[:, :, 0:n], gate[:, 1, :, 0:n], ALU.mult).then_inc(yc_ok.sem, 1)
                pool.wait_ge(yc_ok.sem, yc_ok.at(i, 1))
                y_low(i, n, 4, yc[:, :, 0:n], 1)
                y_low(i, n, 6, gate[:, 2, :, 0:n], 2)
                y_low(i, n, 2, z[:, :, 0:n], 3)
                if len(nxt) > 1:
                    rows_newton(nxt[1][0], nxt[1][1])
                pool.wait_ge(o_v.sem, o_v.at(i, 4))
                newton(o_newton, i, 0, O_V[0:m0, 0:nt], O_Y[0:m0, 0:nt], O_T[0:m0, 0:nt])
                pool.wait_ge(o_rs.sem, o_rs.at(i, 1))
                if first:
                    pool.wait_ge(gf_in.sem, 16)
                for t, _, m in tiles(n):
                    ins = nc.gpsimd.tensor_tensor(ob[0:m, t, :], ob[0:m, t, :], gf[0:m, :], ALU.mult)
                ins.then_inc(o_ok.sem, 1)

            nc.gpsimd.memset(ident[:, :], 0.0).then_inc(ident_ok.sem, 1)
            nc.gpsimd.memset(ones[:, :], 1.0)
            pool.wait_ge(ident_ok.sem, 1)
            nc.gpsimd.affine_select(out=ident[:, :], in_=ident[:, :], compare_op=ALU.not_equal, fill=1.0, base=0,
                                    pattern=[[-1, P]], channel_multiplier=1).then_inc(ident_ok.sem, 1)
            nc.gpsimd.iota(l1[:, 0, 0:32].rearrange("p (c t) -> p c t", c=CT).bitcast(I32), [[0, CT], [1, 16]], base=1,
                           channel_multiplier=0).then_inc(ramp_s.sem, 1)
            pool.wait_ge(ramp_s.sem, 1)
            nc.gpsimd.tensor_copy(ramp[:, :, :], l1[:, 0, 0:32].rearrange("p (c t) -> p c t", c=CT).bitcast(I32)).then_inc(ramp_s.sem, 1)
            pool.wait_ge(zero_ok.sem, 4)
            rows_newton(0, P)
            pool.wait_ge(cev.sem, 1)
            prep(0)
            rows_newton(1, P)
            prep(1)
            rows_newton(2, P)
            rows_newton(3, P)
            prep(2)
            prep(3)

            def next_tiles(i):
                return [(2 * i + 4, P), (2 * i + 5, P)]

            chunk(0, N, next_tiles(0))
            with pool.Fori(1, LAST) as i:
                chunk(i, N, next_tiles(i))
            chunk(LAST, N, [(2 * LAST + 4, SAMPLE)])
            chunk(CHUNKS, SAMPLE, [])


_INS = ["x_prompt", "x_sample", "mem_prompt", "state_conv_a", "state_conv_b", "state_pool", "cache_mem_k",
        "cache_mem_v", "norm_g", "w_in", "conv_a_w", "conv_b_w", "conv_b_bias", "ln_b_g", "ln_b_b", "pool_w",
        "pool_bias", "pool_scale", "mem_norm_g", "w_mem_k", "w_mem_v", "w_out", "final_norm_g"]
_OUTS = [(1, SEQ, D), (1, SAMPLE, D), (1, 1, HA, GW), (1, 1, HB, GW), (1, 1, HP, GW),
         (1, 1, NMEM, HEADS, HD), (1, 1, NMEM, HEADS, HD), (1, 1, HA, GW), (1, 1, HB, GW), (1, 1, HP, GW)]


def kernel(**inputs):
    import numpy as np
    import concourse.bacc as bacc
    from concourse.bass_utils import run_bass_kernel_spmd

    nc = bacc.Bacc("TRN2", target_bir_lowering=False, num_devices=1)
    arrays, args = {}, []
    for name in _INS:
        a = np.ascontiguousarray(inputs[name])
        arrays[f"in_{name}"] = a
        args.append(nc.dram_tensor(f"in_{name}", a.shape, mybir.dt.from_np(a.dtype), kind="ExternalInput").ap())
    for k, shape in enumerate(_OUTS):
        args.append(nc.dram_tensor(f"out_{k}", shape, F32, kind="ExternalOutput").ap())
    encoder_program(nc, *args)
    r = run_bass_kernel_spmd(nc, [arrays], core_ids=[0])
    return tuple(r.results[0][f"out_{k}"] for k in range(len(_OUTS)))
```

```python
from contextlib import ExitStack

import concourse.bass as bass
from concourse import mybir

F32 = mybir.dt.float32
F32R = mybir.dt.float32r
F16 = mybir.dt.float16
BF16 = mybir.dt.bfloat16
I32 = mybir.dt.int32
ACT = mybir.ActivationFunctionType
ALU = mybir.AluOpType
AX = mybir.AxisListType

P = 128
D = 1024
KT = D // P
GW = 256
CT = GW // P
NG = 11
FT = NG * CT
SEQ, SAMPLE = 4096, 64
N = 256
CHUNKS = SEQ // N
LAST = CHUNKS - 1
TA, TB, HP = 3, 31, 15
HA, HB = TA - 1, TB - 1
HEADS, HD, NMEM = 4, 64, 256
PAIRS, MT = HEADS // 2, NMEM // P
WINDOWS = (2, 4, 8, 16)
EPS = 1e-6
HALF = 512

SPLIT = {"a_b": 0, "a_c": 1, "a_x": 2, "a_g": 3, "b_v": 4, "b_a": 5, "b_g": 6, "c_u": 7, "c_g": 8,
         "x_q": 9, "x_g": 10}
ORDER = ["b_a", "b_v", "x_q", "c_u", "a_c", "a_x", "a_b", "a_g", "b_g", "c_g", "x_g"]

SLOTS = ["b_a", "b_v", "x_q", "c_u", "a_c", "a_x", "a_b", "a_g", "mix", "b_g", "zf", "c_g", "x_g",
         "zb", "t0", "t1", "t2", "t3"]
AHEAD, GAINS = 4, 5
FIRST = ["t0", "t1", "t2", "t3", "w0", "w1", "w2"]
for _n, _g in enumerate(ORDER):
    FIRST += {"b_g": ["mix"], "c_g": ["zf"]}.get(_g, []) + [_g]
    FIRST += [f"w{AHEAD - 1}"] if _n == 0 else []
    FIRST += [f"w{_n + AHEAD}"] if _n + AHEAD < NG else []
FIRST += ["zb", "n0", "n1", "n2", "n3"]
NFIRST = len(FIRST)

Y_ORDER = [0, 4, 6, 2]
K_ORDER = [k + c for k in Y_ORDER for c in range(CT)]
PIECES = 2 * KT
RAW, WST = 8, 4

R_AW, R_BW = 0, TA
R_BIAS, R_LNG, R_LNB, R_PB, R_PS = range(TA + TB, TA + TB + 5)
NR = TA + TB + 5

MAGIC = 0x5F3759DF
NEWTON = 3
RSQRT = 4 + 2 * NEWTON
XSCALE = 1024.0
WEXP = 14


def encoder_program(nc, x_prompt, x_sample, mem_prompt, state_conv_a, state_conv_b, state_pool,
                    cache_mem_k, cache_mem_v, norm_g, w_in, conv_a_w, conv_b_w, conv_b_bias, ln_b_g,
                    ln_b_b, pool_w, pool_bias, pool_scale, mem_norm_g, w_mem_k, w_mem_v, w_out,
                    final_norm_g, y_prompt, y_sample, new_a_p, new_b_p, new_c_p, new_k, new_v,
                    new_a_s, new_b_s, new_c_s):
    ctx = ExitStack()
    with ctx:
        def sb(name, shape, dt=F32):
            return ctx.enter_context(nc.sbuf_tensor(name, shape, dt))

        def sem(name):
            return ctx.enter_context(nc.semaphore(name))

        w_hi = sb("w_hi", [P, FT, KT, P], F16)
        w_lo = sb("w_lo", [P, FT, KT, P], F16)
        stage = sb("stage", [P, 2, KT, P])
        raw = stage[:, :, :, :].rearrange("p a b c -> p (a b c)").rearrange("p (s n) -> p s n", n=HALF)
        wo_hi = sb("wo_hi", [P, WST, HALF], F32R)
        wo_lo = sb("wo_lo", [P, WST, HALF], F32R)
        h_hi = sb("h_hi", [P, KT, N], F16)
        h_lo = sb("h_lo", [P, KT, N], F16)
        y_hi = sb("y_hi", [P, KT, N], F32R)
        y_lo = sb("y_lo", [P, KT, N], F32R)
        xb = sb("xb", [P, D])
        ob = sb("ob", [P, 2, D])
        kt_hi = sb("kt_hi", [P, PAIRS, NMEM], F32R)
        kt_lo = sb("kt_lo", [P, PAIRS, NMEM], F32R)
        v_hi = sb("v_hi", [P, MT, PAIRS, 3 * HD], F32R)
        v_lo = sb("v_lo", [P, MT, PAIRS, 3 * HD], F32R)
        probs = sb("probs", [P, 2, 2, NMEM])
        kv = probs[:, :, :, :].rearrange("p b h m -> p b (h m)")
        pt_hi = sb("pt_hi", [P, 2, MT, N], F32R)
        pt_lo = sb("pt_lo", [P, 2, MT, N], F32R)
        glu = sb("glu", [P, CT, HB + N])
        va = sb("va", [P, CT, HA + N])
        cu = sb("cu", [P, CT, HP + N])
        z = sb("z", [P, CT, N])
        ya = sb("ya", [P, CT, N])
        yc = sb("yc", [P, CT, N])
        gate = sb("gate", [P, 3, CT, N])
        dq_hi = sb("dq_hi", [P, CT, N], F32R)
        dq_lo = sb("dq_lo", [P, CT, N], F32R)
        S2, S4 = HP - 1, HP - 3
        sa = sb("sa", [P, CT, S2 + N])
        sb_ = sb("sb4", [P, CT, S4 + N])
        zt = sa[:, :, :].rearrange("p a b -> p (a b)")[:, 0:2 * GW].rearrange("p (t c) -> p t c", t=2)
        junk = sb("junk", [P, D], BF16)
        raws = [raw[:, b, :] for b in range(4)] + [kv[:, b, :] for b in range(MT)] + [
            win[:, :, :].rearrange("p a b -> p (a b)")[:, 0:HALF] for win in (sb_, sa)]
        kv_s = gate[:, 0:MT, :, :].rearrange("p b c n -> p b (c n)")
        pw_hi = sb("pw_hi", [P, CT, P], F32R)
        pw_lo = sb("pw_lo", [P, CT, P], F32R)
        gf = sb("gf", [P, D])
        l1 = gf[:, :].rearrange("p (s n) -> p s n", s=4)
        mags = ob[:, 1, :].bitcast(BF16).rearrange("p (b k n) -> p b k n", b=2, n=P)
        ident = sb("ident", [P, P])
        ones = sb("ones", [P, P], BF16)
        cst = sb("cst", [P, CT, NR])
        pbs = sb("pbs", [P, CT])
        gcol = sb("gcol", [P, 2 * KT])
        inv = sb("inv", [P, FT])
        ramp = sb("ramp", [P, CT, 16])
        st = sb("st", [P, 96])
        (X_SQ, X_V, X_SH, X_Y), (O_SQ, O_V, O_SH, O_Y), (L_V, L_SH, L_Y) = (
            [st[:, 2 * (a + b):2 * (a + b) + 2] for b in range(m)] for a, m in ((0, 4), (4, 4), (8, 3)))
        nmax, rsum, rcp = (st[:, 28 + 8 * a:36 + 8 * a].rearrange("p (s h) -> p s h", h=2) for a in range(3))
        bn6 = st[:, 52:64].rearrange("p (t s) -> p t s", t=2)
        mv = st[:, 64:68].rearrange("p (t s) -> p t s", t=2)

        U = [ctx.enter_context(nc.psum_tensor(f"u{b}", [P, HALF], F32)) for b in range(3)]
        sps = ctx.enter_context(nc.psum_tensor("sps", [P, 2, HALF], F32))
        qps = ctx.enter_context(nc.psum_tensor("qps", [P, 2, HALF], F32))
        ops = ctx.enter_context(nc.psum_tensor("ops", [P, HALF], F32))
        mem_t = [sps[:, 0, :], sps[:, 1, :], qps[:, 0, :], qps[:, 1, :]]

        class Signal:
            def __init__(self, name, per):
                self.sem, self.per = sem(name), per

            def at(self, i, k):
                return i * self.per + k

        def signal(name, per=1):
            return Signal(name, per)

        def needed(value):
            return type(value) is not int or value > 0

        c_in, ident_ok, consts_ok, ctr, cev, pw_in, pw_ok = (
            signal(n) for n in ("c_in", "ident_ok", "consts_ok", "ctr", "cev", "pw_in", "pw_ok"))
        ramp_s, zero_ok, gf_in = signal("ramp_s"), signal("zero_ok"), signal("gf_in")
        mt_ready = signal("mt_ready")
        first_in = [signal(f"first_in{j}") for j in range(4)]
        w_in_ok = [signal(f"w_in_ok{g}") for g in range(NG)]
        wg_ok, mags_ok, l1_s, scaled0, scaled1, whi_ok, wlo0_ok, wlo1_ok = (
            signal(n) for n in ("wg_ok", "mags_ok", "l1_s", "scaled0", "scaled1", "whi_ok", "wlo0_ok", "wlo1_ok"))
        kw_in = [signal(f"kw_in{b}") for b in range(4)]
        mn_hi, mn_lo, kw_hi, kw_lo, kvp, kv_ok, kv_in, ktp, kt_h, kt_l, v_h, v_l = (
            signal(n) for n in ("mn_hi", "mn_lo", "kw_hi", "kw_lo", "kvp", "kv_ok", "kv_in", "ktp",
                                "kt_h", "kt_l", "v_h", "v_l"))
        st_in, stp, st_ok, stored_st = (signal(n) for n in ("st_in", "stp", "st_ok", "stored_st"))
        x_in = signal("x_in", 32)
        x_sq, x_v, x_scaled = signal("x_sq", 2), signal("x_v", 2 * RSQRT), signal("x_scaled", 2)
        h_hi_ok, h_lo_ok = signal("h_hi_ok", 4), signal("h_lo_ok", 4)
        u_ready = signal("u_ready", len(SLOTS))
        s_ready, pt_ready, pv_ready, o_piece = signal("s_ready", 2), signal("pt_ready", 2), signal("pv_ready", 2), signal("o_piece", PIECES)
        hist_ok, sig_ok, glu_ok, conv_step = signal("hist_ok", 3), signal("sig_ok"), signal("glu_ok"), signal("conv_step", 2 * TB)
        bn_s, ln_v, zt_ok, zs_ok, bg_ok, yb_ok = (
            signal("bn_s", 2), signal("ln_v", RSQRT + 2 * NEWTON), signal("zt_ok"),
            signal("zs_ok"), signal("bg_ok"), signal("yb_ok"))
        ac_ok, va_ok, conv_a, ag_ok, ya_ok = signal("ac_ok"), signal("va_ok"), signal("conv_a", 4 * CT), signal("ag_ok"), signal("ya_ok")
        cu_ok, win_ok, d_ok, d_hi, d_lo, mix_ok, cg_ok, yc_ok = (
            signal("cu_ok"), signal("win_ok", 4), signal("d_ok"), signal("d_hi"), signal("d_lo"),
            signal("mix_ok"), signal("cg_ok"), signal("yc_ok"))
        q_hi, q_lo, nmax_ok, exp_ok, rcp_ok, p_ok = (
            signal("q_hi"), signal("q_lo"), signal("nmax_ok", 2), signal("exp_ok", 4), signal("rcp_ok", 4), signal("p_ok", 4))
        pt_hi_ok, pt_lo_ok, xg_ok, yx_ok = signal("pt_hi_ok", 4), signal("pt_lo_ok", 4), signal("xg_ok"), signal("yx_ok")
        y_hi_ok, y_lo_ok = signal("y_hi_ok", 4), signal("y_lo_ok", 4)
        raw_in = [signal(f"raw_in{b}", 16 * PIECES // RAW) for b in range(RAW)]
        wo_hi_ok, wo_lo_ok = signal("wo_hi_ok", PIECES), signal("wo_lo_ok", PIECES)
        res_in, stored = [signal(f"res_in{t}", 16) for t in range(2)], [signal(f"stored{t}", 16) for t in range(2)]
        r_ok, o_sq, o_v, o_ok = signal("r_ok", 4), signal("o_sq", 2), signal("o_v", RSQRT + 2 * NEWTON), signal("o_ok")

        def slot(i, name):
            if type(i) is int and i == 0:
                n = FIRST.index(name)
                return n + 1, U[n % 3]
            k = SLOTS.index(name)
            if type(i) is int and i == CHUNKS:
                return NFIRST + len(SLOTS) * (CHUNKS - 1) - 2 + k + 1, U[(NFIRST - 2 + k) % 3]
            return (i - 1) * len(SLOTS) + NFIRST + k + 1, U[(NFIRST + k) % 3]

        EMPTIED = {"b_a": (sig_ok, 1), "b_v": (glu_ok, 1), "x_q": (q_lo, 1), "c_u": (cu_ok, 1),
                   "a_c": (ac_ok, 1), "a_x": (va_ok, 1), "a_b": (conv_a, 4 * CT), "a_g": (ag_ok, 1),
                   "mix": (mix_ok, 1), "b_g": (bg_ok, 1), "zf": (zt_ok, 1), "c_g": (cg_ok, 1),
                   "x_g": (xg_ok, 1), "zb": (zs_ok, 1)}
        EMPTIED |= {f"w{g}": (l1_s, 5 * g + 1) for g in range(NG)}

        def emptied(i, name):
            if type(i) is int and i == 0:
                n = FIRST.index(name) - 3
                if n < 0:
                    return None
                name, j = FIRST[n], 0
                if name[0] == "n":
                    name, j = "t" + name[1], 1
            else:
                k = SLOTS.index(name)
                order = SLOTS[:-2] if type(i) is int and i == CHUNKS else SLOTS
                if k >= 3:
                    name, j = SLOTS[k - 3], i + (SLOTS[k - 3] in ("t0", "t1", "t2", "t3"))
                else:
                    name = order[k - 3]
                    j = i if name[0] == "t" else i - 1
            if name[0] == "t" and name[1:].isdigit():
                return h_lo_ok.sem, h_lo_ok.at(j, int(name[1]) + 1)
            s, c = EMPTIED[name]
            return s.sem, s.at(j, c)

        def tiles(n):
            return [(t, t * P, min(P, n - t * P)) for t in range((n + P - 1) // P)]

        w_in_v = w_in[0].rearrange("(k p) (f c) -> f p k c", p=P, c=P)
        w_out_v = w_out[0].rearrange("(k p) (h c) -> h k p c", p=P, c=HALF)

        def pos(name):
            return ORDER.index(name) * CT

        def w_raw(j):
            g = j // CT + 1
            if g == NG:
                return stage[:, j % 2]
            return (w_hi, w_lo)[j % 2][:, CT * g:CT * g + CT].rearrange("p a k c -> p (a k c)").bitcast(F32).rearrange(
                "p (k c) -> p k c", c=P)

        block = ctx.enter_context(nc.Block())

        @block.sync
        def _(sp):
            sp.dma_start(ob[:, 0, :], x_prompt[0, 0:P, :]).then_inc(first_in[0].sem, 16)
            sp.dma_start(z[0:TA, 0, :], conv_a_w[0]).then_inc(c_in.sem, 16)
            sp.dma_start(z[R_BW:R_BW + TB, 0, :], conv_b_w[0]).then_inc(c_in.sem, 16)
            for r, v in ((R_BIAS, conv_b_bias), (R_LNG, ln_b_g), (R_LNB, ln_b_b), (R_PB, pool_bias), (R_PS, pool_scale)):
                sp.dma_start(z[r:r + 1, 0, :], v).then_inc(c_in.sem, 16)
            sp.dma_start(z[0:KT, 1, 0:P], norm_g[0].rearrange("(k p) -> k p", p=P)).then_inc(c_in.sem, 16)
            sp.dma_start(z[KT:2 * KT, 1, 0:P], mem_norm_g[0].rearrange("(k p) -> k p", p=P)).then_inc(c_in.sem, 16)
            sp.dma_start(ob[:, 1, :], x_prompt[0, P:2 * P, :]).then_inc(first_in[1].sem, 16)

            def load_split(g):
                for c in range(CT):
                    sp.dma_start(w_raw(CT * g + c), w_in_v[CT * SPLIT[ORDER[g]] + c]).then_inc(w_in_ok[g].sem, 16)

            def load_memory_weights(k):
                if k >= 4:
                    sp.wait_ge(kw_lo.sem, k - 3)
                sp.dma_start(raw[:, k % 4, 0:GW], w_mem_k[0, k * P:(k + 1) * P, :]).then_inc(kw_in[k % 4].sem, 16)
                sp.dma_start(raw[:, k % 4, GW:2 * GW], w_mem_v[0, k * P:(k + 1) * P, :]).then_inc(kw_in[k % 4].sem, 16)

            load_split(0)
            sp.dma_start(xb[:, :], mem_prompt[0, 0:P, :]).then_inc(first_in[2].sem, 16)
            load_split(1)
            sp.wait_ge(u_ready.sem, FIRST.index("t1") + 1)
            sp.dma_start(ob[:, 0, :], mem_prompt[0, P:2 * P, :]).then_inc(first_in[3].sem, 16)
            for k in range(4):
                load_memory_weights(k)
            load_split(2)
            sp.wait_ge(zero_ok.sem, 1)
            for g in range(4):
                q = (g % 2) * HD
                sp.dma_start(ya[q:q + HD, 0, (g // 2) * P + q:(g // 2) * P + q + HD], pool_w[0, g]).then_inc(pw_in.sem, 16)
            load_split(3)
            load_split(4)
            for k in range(4, KT):
                load_memory_weights(k)
            sp.wait_ge(mt_ready.sem, 2)
            sp.dma_start(xb[:, :], x_prompt[0, 2 * P:3 * P, :]).then_inc(x_in.sem, 16)
            for g in range(5, NG):
                if g == NG - 1:
                    sp.wait_ge(kw_lo.sem, KT)
                load_split(g)
            sp.wait_ge(kv_ok.sem, 2)
            for dst, off in ((new_k, 0), (new_v, GW)):
                sp.dma_start(dst[0, 0].rearrange("(t p) h d -> p t (h d)", p=P), kv[:, :, off:off + GW]).then_inc(kv_in.sem, 16)

            def store_states(k, outs):
                sp.wait_ge(st_ok.sem, 2 * k + 2)
                (a, b, c) = outs
                sp.dma_start(b[0, 0], ya[0:HB, 0, :]).then_inc(stored_st.sem, 16)
                sp.dma_start(c[0, 0], ya[0:HP, 1, :]).then_inc(stored_st.sem, 16)
                sp.dma_start(a[0, 0], yc[0:HA, 0, :]).then_inc(stored_st.sem, 16)

            def sync_chunk(i, n, x_here, y_here, x_next, x_after):
                if type(i) is int and i == 0:
                    sp.wait_ge(wlo0_ok.sem, NG)
                    sp.wait_ge(wlo1_ok.sem, NG)
                    sp.dma_start(gf[:, :], final_norm_g.partition_broadcast(P)).then_inc(gf_in.sem, 16)
                for t, _, m in tiles(n):
                    if not (type(i) is int and i == 0):
                        sp.wait_ge(stored[t].sem, stored[t].at(i, 0))
                    sp.dma_start(ob[0:m, t, :], x_here[t]).then_inc(res_in[t].sem, 16)
                for q in range(PIECES):
                    if q == 4:
                        sp.wait_ge(pt_ready.sem, pt_ready.at(i, 2))
                    elif q == 6:
                        sp.wait_ge(d_ok.sem, d_ok.at(i, 1))
                    elif q == 7:
                        sp.wait_ge(u_ready.sem, slot(i, "zb")[0])
                    elif q >= RAW or q < 4 and not (type(i) is int and i == 0):
                        sp.wait_ge(wo_lo_ok.sem, wo_lo_ok.at(i, q - RAW + 1))
                    half, k = q // KT, K_ORDER[q % KT]
                    sp.dma_start(raws[q % RAW], w_out_v[half, k]).then_inc(raw_in[q % RAW].sem, 16)
                    if type(i) is int and i == LAST and q == KT:
                        sp.wait_ge(y_lo_ok.sem, y_lo_ok.at(LAST, 4))
                        for src, off in ((cache_mem_k, 0), (cache_mem_v, GW)):
                            sp.dma_start(kv_s[:, :, off:off + GW], src[0, 0].rearrange("(t p) h d -> p t (h d)", p=P)).then_inc(kv_in.sem, 16)
                        sp.dma_start(z[0:HB, 0, :], state_conv_b[0, 0]).then_inc(st_in.sem, 16)
                        sp.dma_start(z[0:HP, 1, :], state_pool[0, 0]).then_inc(st_in.sem, 16)
                        sp.dma_start(yc[0:HA, 1, :], state_conv_a[0, 0]).then_inc(st_in.sem, 16)
                    if q == 8 and x_next is not None:
                        v = NFIRST - 2 if type(i) is int and i == 0 else i * len(SLOTS) + NFIRST - 2
                        sp.wait_ge(u_ready.sem, v)
                        sp.dma_start(xb[:, :], x_next).then_inc(x_in.sem, 16)
                if x_after is not None:
                    sp.wait_ge(u_ready.sem, i * len(SLOTS) + NFIRST)
                    sp.dma_start(xb[0:x_after.shape[0], :], x_after).then_inc(x_in.sem, 16)
                if type(i) is int and i >= LAST:
                    store_states(i - LAST, ((new_a_p, new_b_p, new_c_p), (new_a_s, new_b_s, new_c_s))[i - LAST])
                sp.wait_ge(o_ok.sem, o_ok.at(i, 1))
                for t, _, m in tiles(n):
                    sp.dma_start(y_here[t], ob[0:m, t, :]).then_inc(stored[t].sem, 16)

            def prompt_chunk(i, here, nxt, after):
                sync_chunk(i, N, [x_prompt[0, bass.ds(h, P), :] for h in here], [y_prompt[0, bass.ds(h, P), :] for h in here],
                           x_prompt[0, bass.ds(nxt, P), :] if nxt is not None else None,
                           x_prompt[0, bass.ds(after, P), :] if after is not None else x_sample[0] if nxt is not None else None)

            prompt_chunk(0, [0, P], N + P, 2 * N)
            with sp.Fori(1, LAST - 1) as i:
                h0, h1, nx, af = (sp.snap(i * N + t) for t in (0, P, N + P, 2 * N))
                prompt_chunk(i, [h0, h1], nx, af)
            prompt_chunk(LAST - 1, [(LAST - 1) * N, (LAST - 1) * N + P], LAST * N + P, None)
            prompt_chunk(LAST, [LAST * N, LAST * N + P], None, None)

            sync_chunk(CHUNKS, SAMPLE, [x_sample[0, :, :]], [y_sample[0, :, :]], None, None)
            sp.wait_ge(stored_st.sem, 96)
            sp.wait_ge(kv_in.sem, 64)
            sp.wait_ge(stored[0].sem, stored[0].at(CHUNKS + 1, 0))
            sp.wait_ge(stored[1].sem, stored[1].at(CHUNKS, 0))

        @block.tensor
        def _(pe):
            def three(out, a_hi, a_lo, b_hi, b_lo, first, last):
                nc.tensor.matmul(out, a_hi, b_hi, start=first, stop=False)
                nc.tensor.matmul(out, a_hi, b_lo, start=False, stop=False)
                return nc.tensor.matmul(out, a_lo, b_hi, start=False, stop=last)

            def transposes(i, names, j, rows=xb):
                m = j[1]
                pe.wait_ge(x_scaled.sem, j[0] + 1)
                for h, name in enumerate(names):
                    free = emptied(i, name)
                    if free:
                        pe.wait_ge(*free)
                    _, bank = slot(i, name)
                    for k in range(4):
                        c = (4 * h + k) * P
                        ins = nc.tensor.transpose(bank[:, k * P:k * P + m], rows[0:m, c:c + P], ident[0:m, 0:m])
                    ins.then_inc(u_ready.sem, 1)

            def weight_sums(g):
                free = emptied(0, f"w{g}")
                if free:
                    pe.wait_ge(*free)
                _, bank = slot(0, f"w{g}")
                pe.wait_ge(mags_ok.sem, CT * (g + 1))
                for k in range(KT):
                    ins = nc.tensor.matmul(bank[:, 0:CT * P], ones[:, :], mags[:, :, k, :], start=k == 0, stop=k == KT - 1)
                ins.then_inc(u_ready.sem, 1)

            def project(i, n, name):
                free = emptied(i, name)
                if free:
                    pe.wait_ge(*free)
                _, bank = slot(i, name)
                if name == ORDER[0]:
                    pe.wait_ge(h_lo_ok.sem, h_lo_ok.at(i, 4 if n == N else 2))
                if type(i) is int and i == 0:
                    pe.wait_ge(wlo0_ok.sem, ORDER.index(name) + 1)
                    pe.wait_ge(wlo1_ok.sem, ORDER.index(name) + 1)
                for c in range(CT):
                    for k in range(KT):
                        f = pos(name) + c
                        ins = three(bank[:, c * N:c * N + n], w_hi[:, f, k, :], w_lo[:, f, k, :],
                                    h_hi[:, k, 0:n], h_lo[:, k, 0:n], k == 0, k == KT - 1)
                ins.then_inc(u_ready.sem, 1)

            def scores(i, n, p):
                nt = len(tiles(n))
                if p == 0:
                    pe.wait_ge(q_lo.sem, q_lo.at(i, 1))
                    if not (type(i) is int and i == 0):
                        pe.wait_ge(r_ok.sem, r_ok.at(i, -2))
                        if type(i) is int and i == CHUNKS:
                            pe.wait_ge(st_ok.sem, 2)
                else:
                    pe.wait_ge(exp_ok.sem, exp_ok.at(i, nt))
                for t, t0, m in tiles(n):
                    for h in range(2):
                        r = slice(h * HD, (h + 1) * HD)
                        ins = three(sps[0:m, h, t * NMEM:(t + 1) * NMEM], dq_hi[r, p, t0:t0 + m], dq_lo[r, p, t0:t0 + m],
                                    kt_hi[r, p, :], kt_lo[r, p, :], True, True)
                ins.then_inc(s_ready.sem, 1)

            def probs_t(i, n, p):
                nt = len(tiles(n))
                if p == 0:
                    if not (type(i) is int and i == 0):
                        pe.wait_ge(r_ok.sem, r_ok.at(i, 0))
                else:
                    pe.wait_ge(pt_lo_ok.sem, pt_lo_ok.at(i, 2))
                pe.wait_ge(p_ok.sem, p_ok.at(i, (p + 1) * nt))
                for t, t0, m in tiles(n):
                    b = (p * nt + t) % 2
                    for h in range(2):
                        for k in range(MT):
                            ins = nc.tensor.transpose(qps[:, h, k * N + t0:k * N + t0 + m],
                                                      probs[0:m, b, h, k * P:(k + 1) * P], ident[0:m, 0:m])
                ins.then_inc(pt_ready.sem, 1)

            def attend(i, n, p):
                if p == 0:
                    if needed(yx_ok.at(i, 0)):
                        pe.wait_ge(yx_ok.sem, yx_ok.at(i, 0))
                pe.wait_ge(pt_lo_ok.sem, pt_lo_ok.at(i, 2 * p + 2))
                for h in range(2):
                    for k in range(MT):
                        v = slice(h * HD, h * HD + P)
                        ins = three(ops[:, p * N:p * N + n], v_hi[:, k, p, v], v_lo[:, k, p, v],
                                    pt_hi[:, h, k, 0:n], pt_lo[:, h, k, 0:n],
                                    (h, k) == (0, 0), (h, k) == (1, MT - 1))
                ins.then_inc(pv_ready.sem, 1)

            def mix(i, n):
                free = emptied(i, "mix")
                if free:
                    pe.wait_ge(*free)
                _, bank = slot(i, "mix")
                pe.wait_ge(d_lo.sem, d_lo.at(i, 1))
                if type(i) is int and i == 0:
                    pe.wait_ge(pw_ok.sem, 2)
                for c in range(CT):
                    ins = three(bank[:, c * N:c * N + n], pw_hi[:, c, :], pw_lo[:, c, :],
                                dq_hi[:, c, 0:n], dq_lo[:, c, 0:n], True, True)
                ins.then_inc(u_ready.sem, 1)

            def z_rows(i, n):
                free = emptied(i, "zf")
                if free:
                    pe.wait_ge(*free)
                _, bank = slot(i, "zf")
                pe.wait_ge(conv_step.sem, conv_step.at(i, 2 * TB))
                for t, t0, m in tiles(n):
                    for c in range(CT):
                        ins = nc.tensor.transpose(bank[0:m, t * GW + c * P:t * GW + (c + 1) * P],
                                                  z[:, c, t0:t0 + m], ident[:, :])
                ins.then_inc(u_ready.sem, 1)

            def z_back(i, n):
                free = emptied(i, "zb")
                if free:
                    pe.wait_ge(*free)
                _, bank = slot(i, "zb")
                pe.wait_ge(zt_ok.sem, zt_ok.at(i, 1))
                for t, t0, m in tiles(n):
                    for c in range(CT):
                        ins = nc.tensor.transpose(bank[:, c * N + t0:c * N + t0 + m],
                                                  zt[0:m, t, c * P:(c + 1) * P], ident[0:m, 0:m])
                ins.then_inc(u_ready.sem, 1)

            def out_half(i, n, half, nxt=None):
                banks = sps if half == 0 else qps
                if half == 0:
                    pe.wait_ge(exp_ok.sem, exp_ok.at(i, 4 if n == N else 2))
                else:
                    pe.wait_ge(pt_lo_ok.sem, pt_lo_ok.at(i, 4))
                for a in range(KT):
                    q = half * KT + a
                    if half == 0 and a % CT == 0:
                        pe.wait_ge(y_lo_ok.sem, y_lo_ok.at(i, a // CT + 1))
                    pe.wait_ge(wo_lo_ok.sem, wo_lo_ok.at(i, q + 1))
                    k, s = K_ORDER[a], q % WST
                    for t, t0, m in tiles(n):
                        ins = three(banks[0:m, t, :], y_hi[:, k, t0:t0 + m], y_lo[:, k, t0:t0 + m],
                                    wo_hi[:, s, :], wo_lo[:, s, :], a == 0, a == KT - 1)
                    ins.then_inc(o_piece.sem, 1)
                    if half == 1 and a == 5 and type(i) is int and i == LAST:
                        keys_t(1)
                    if nxt and a == 5:
                        transposes(i, *nxt)

            def keys_t(k):
                if k == 0:
                    pe.wait_ge(kv_ok.sem, 2)
                else:
                    pe.wait_ge(kv_in.sem, 64)
                    pe.wait_ge(yx_ok.sem, yx_ok.at(LAST, 1))
                for p in range(PAIRS):
                    for t in range(MT):
                        ins = nc.tensor.transpose(ops[:, p * NMEM + t * P:p * NMEM + (t + 1) * P],
                                                  (kv, kv_s)[k][:, t, p * P:(p + 1) * P], ident[:, :])
                ins.then_inc(ktp.sem, 1)

            def memory_transposes(t, rows):
                pe.wait_ge(x_scaled.sem, 2 + t + 1)
                for h in range(2):
                    for k in range(4):
                        c = (4 * h + k) * P
                        ins = nc.tensor.transpose(mem_t[2 * t + h][:, k * P:(k + 1) * P], rows[:, c:c + P], ident[:, :])
                    ins.then_inc(mt_ready.sem, 1)

            def memory_products():
                pe.wait_ge(mn_lo.sem, 4)
                for k in range(KT):
                    pe.wait_ge(kw_lo.sem, k + 1)
                    for t in range(MT):
                        ins = three(sps[:, t, :], y_hi[:, k, t * P:(t + 1) * P], y_lo[:, k, t * P:(t + 1) * P],
                                    wo_hi[:, k % WST, :], wo_lo[:, k % WST, :], k == 0, k == KT - 1)
                    ins.then_inc(kvp.sem, 1)

            def chunk(i, n, nxt):
                first = type(i) is int and i == 0

                def prj(name):
                    project(i, n, name)
                    g = ORDER.index(name) + AHEAD
                    if first and g < NG:
                        weight_sums(g)

                project(i, n, "b_a")
                if first:
                    weight_sums(AHEAD - 1)
                    memory_products()
                    weight_sums(AHEAD)
                prj("b_v")
                if first:
                    keys_t(0)
                prj("x_q")
                prj("c_u")
                if first:
                    pe.wait_ge(kt_l.sem, 1)
                    pe.wait_ge(v_l.sem, 1)
                scores(i, n, 0)
                prj("a_c")
                probs_t(i, n, 0)
                scores(i, n, 1)
                prj("a_x")
                attend(i, n, 0)
                prj("a_b")
                probs_t(i, n, 1)
                prj("a_g")
                attend(i, n, 1)
                mix(i, n)
                prj("b_g")
                z_rows(i, n)
                prj("c_g")
                prj("x_g")
                z_back(i, n)
                if nxt:
                    transposes(i, *nxt[0])
                out_half(i, n, 0)
                out_half(i, n, 1, nxt[1] if len(nxt) > 1 else None)

            def states_out(n):
                for src, ln, b, off in ((glu, HB, 0, 0), (cu, HP, 0, GW), (va, HA, 1, 0)):
                    for c in range(CT):
                        ins = nc.tensor.transpose(sps[0:ln, b, off + c * P:off + (c + 1) * P],
                                                  src[:, c, n:n + ln], ident[:, :])
                ins.then_inc(stp.sem, 1)

            pe.wait_ge(ident_ok.sem, 2)
            pe.wait_ge(c_in.sem, 16 * 9)
            for c in range(CT):
                nc.tensor.transpose(ops[:, c * NR:(c + 1) * NR], z[0:NR, 0, c * P:(c + 1) * P], ident[0:NR, 0:NR])
            nc.tensor.transpose(ops[:, CT * NR:CT * NR + 2 * KT], z[0:2 * KT, 1, 0:P],
                                ident[0:2 * KT, 0:2 * KT]).then_inc(ctr.sem, 1)
            transposes(0, ("t0", "t1"), (0, P), ob[:, 0])
            transposes(0, ("t2", "t3"), (1, P), ob[:, 1])
            weight_sums(0)
            weight_sums(1)
            memory_transposes(0, xb)
            memory_transposes(1, ob[:, 0])
            weight_sums(2)

            def next_tiles(i, names=("t0", "t1", "t2", "t3")):
                return [(names[0:2], (2 * i + 4, P)), (names[2:4], (2 * i + 5, P))]

            chunk(0, N, next_tiles(0, ("n0", "n1", "n2", "n3")))
            with pe.Fori(1, LAST) as i:
                chunk(i, N, next_tiles(i))
            chunk(LAST, N, [(("t0", "t1"), (2 * LAST + 4, SAMPLE))])
            states_out(N)
            pe.wait_ge(kt_l.sem, 2)
            pe.wait_ge(st_in.sem, 48)
            for c in range(CT):
                nc.tensor.transpose(ops[:, c * P:c * P + HB], z[0:HB, 0, c * P:(c + 1) * P], ident[0:HB, 0:HB])
                nc.tensor.transpose(ops[:, c * P + 32:c * P + 32 + HP], z[0:HP, 1, c * P:(c + 1) * P], ident[0:HP, 0:HP])
                ins = nc.tensor.transpose(ops[:, c * P + 64:c * P + 64 + HA], yc[0:HA, 1, c * P:(c + 1) * P], ident[0:HA, 0:HA])
            ins.then_inc(stp.sem, 1)
            pe.wait_ge(v_l.sem, 2)
            pe.wait_ge(hist_ok.sem, hist_ok.at(CHUNKS, 3))
            chunk(CHUNKS, SAMPLE, [])
            pe.wait_ge(r_ok.sem, r_ok.at(CHUNKS, 2))
            states_out(SAMPLE)

        @block.scalar
        def _(act):
            def at(i, name):
                n, bank = slot(i, name)
                act.wait_ge(u_ready.sem, n)
                return bank[:, :].rearrange("p (c n) -> p c n", c=CT)

            def scaled_out(i, n, name, dst, func, s):
                u = at(i, name)
                for c in range(CT):
                    f = pos(name) + c
                    ins = nc.scalar.activation(dst[:, c], u[:, c, 0:n], func, scale=inv[:, f:f + 1])
                ins.then_inc(s.sem, 1)

            def squares(j, m, i=0, rows=xb, loaded=None):
                act.wait_ge(loaded or x_in.sem, 16 if loaded else 16 * (j - 3))
                if needed(j):
                    act.wait_ge(x_v.sem, RSQRT * j)
                if needed(o_sq.at(i, 0)):
                    act.wait_ge(o_sq.sem, o_sq.at(i, 0))
                nc.scalar.activation(junk[0:m, :], rows[0:m, :], ACT.Square,
                                     accum_out=X_SQ[0:m, 0:1]).then_inc(x_sq.sem, 1)

            def rows_hi(i, names, j, t, m):
                for h, name in enumerate(names):
                    n, bank = slot(i, name)
                    act.wait_ge(u_ready.sem, n)
                    src = bank[:, :].rearrange("p (k c) -> p k c", k=4)[:, :, 0:m]
                    nc.scalar.activation(h_hi[:, 4 * h:4 * h + 4, t * P:t * P + m], src, ACT.Copy).then_inc(h_hi_ok.sem, 1)

            def piece_hi(i, q):
                act.wait_ge(raw_in[q % RAW].sem, raw_in[q % RAW].at(i, 16 * (q // RAW + 1)))
                if needed(o_piece.at(i, q - WST + 1)):
                    act.wait_ge(o_piece.sem, o_piece.at(i, q - WST + 1))
                nc.scalar.activation(wo_hi[:, q % WST, :], raws[q % RAW], ACT.Copy).then_inc(wo_hi_ok.sem, 1)

            def magnitudes(g):
                if g:
                    act.wait_ge(u_ready.sem, FIRST.index(f"w{g - 1}") + 1)
                else:
                    act.wait_ge(u_ready.sem, FIRST.index("t3") + 1)
                for j in (CT * g, CT * g + 1):
                    act.wait_ge(wg_ok.sem, j + 1)
                    nc.scalar.activation(mags[:, j % 2], w_raw(j), ACT.Abs).then_inc(mags_ok.sem, 1)

            def w_high(g):
                for c, s in enumerate((scaled0, scaled1)):
                    act.wait_ge(s.sem, g + 1)
                    if g:
                        act.wait_ge(wlo0_ok.sem, g)
                    nc.scalar.activation(w_hi[:, CT * g + c], w_raw(CT * g + c), ACT.Copy).then_inc(whi_ok.sem, 1)

            def exps(i, n, p):
                nt = len(tiles(n))
                for t, t0, m in tiles(n):
                    s = p * nt + t
                    b = s % 2
                    act.wait_ge(nmax_ok.sem, nmax_ok.at(i, p + 1))
                    if s >= 2:
                        act.wait_ge(pt_ready.sem, pt_ready.at(i, (s - 2) // nt + 1))
                    elif type(i) is int and i == 0:
                        act.wait_ge(kv_in.sem, 32)
                        act.wait_ge(v_l.sem, 1)
                    else:
                        act.wait_ge(pt_ready.sem, pt_ready.at(i, 0))
                        if type(i) is int and i == CHUNKS:
                            act.wait_ge(v_l.sem, 2)
                    for h in range(2):
                        ins = nc.scalar.activation(probs[0:m, b, h, :], sps[0:m, h, t * NMEM:(t + 1) * NMEM], ACT.Exp,
                                                   bias=nmax[0:m, s, h:h + 1], scale=1.0,
                                                   accum_out=rsum[0:m, s, h:h + 1])
                    ins.then_inc(exp_ok.sem, 1)

            def probs_hi(i, n, p):
                act.wait_ge(pt_ready.sem, pt_ready.at(i, p + 1))
                if needed(pv_ready.at(i, p)):
                    act.wait_ge(pv_ready.sem, pv_ready.at(i, p))
                for h in range(2):
                    src = qps[:, h, :].rearrange("p (k n) -> p k n", k=MT)[:, :, 0:n]
                    nc.scalar.activation(pt_hi[:, h, :, 0:n], src, ACT.Copy).then_inc(pt_hi_ok.sem, 1)

            def y_high(i, n, k, src, s):
                act.wait_ge(s.sem, s.at(i, 1))
                nc.scalar.activation(y_hi[:, k:k + CT, 0:n], src, ACT.Copy).then_inc(y_hi_ok.sem, 1)

            def keys_values_hi(k):
                act.wait_ge(ktp.sem, k + 1)
                if k == 1:
                    act.wait_ge(pv_ready.sem, pv_ready.at(LAST, 2))
                if k == 0:
                    act.wait_ge(zero_ok.sem, 3)
                nc.scalar.activation(kt_hi[:, :, :], ops[:, :].rearrange("p (a m) -> p a m", a=PAIRS), ACT.Copy,
                                     scale=HD ** -0.5).then_inc(kt_h.sem, 1)
                for t in range(MT):
                    src = (kv, kv_s)[k][:, t, GW:2 * GW].rearrange("p (a h d) -> p a h d", a=PAIRS, h=2)
                    dst = v_hi[:, t].rearrange("p a (s d) -> p a s d", s=3)[:, :, 0::2, :]
                    ins = nc.scalar.activation(dst, src, ACT.Copy)
                ins.then_inc(v_h.sem, 1)

            def states_ok(k):
                act.wait_ge(stp.sem, 2 * k + 1)
                nc.scalar.activation(ya[0:HB, 0, :], sps[0:HB, 0, 0:GW], ACT.Copy)
                nc.scalar.activation(ya[0:HP, 1, :], sps[0:HP, 0, GW:2 * GW], ACT.Copy).then_inc(st_ok.sem, 1)
                nc.scalar.activation(yc[0:HA, 0, :], sps[0:HA, 1, 0:GW], ACT.Copy).then_inc(st_ok.sem, 1)

            def memory_hi(t):
                for h in range(2):
                    bank = mem_t[2 * t + h]
                    act.wait_ge(mt_ready.sem, 2 * t + h + 1)
                    for k in range(4):
                        kk = 4 * h + k
                        ins = nc.scalar.activation(y_hi[:, kk, t * P:(t + 1) * P], bank[:, k * P:(k + 1) * P], ACT.Copy,
                                                   scale=gcol[:, KT + kk:KT + kk + 1])
                    ins.then_inc(mn_hi.sem, 1)

            def kw(k):
                b = k % 4
                act.wait_ge(kw_in[b].sem, 32 * (k // 4 + 1))
                if needed(k - WST + 1):
                    act.wait_ge(kvp.sem, k - WST + 1)
                nc.scalar.activation(wo_hi[:, k % WST, :], raw[:, b, :], ACT.Copy).then_inc(kw_hi.sem, 1)

            def chunk(i, n, nxt):
                first = type(i) is int and i == 0

                def prepare(g):
                    if first:
                        w_high(g + AHEAD - 1)
                        if g + AHEAD + 1 < NG:
                            magnitudes(g + AHEAD + 1)

                if needed(y_lo_ok.at(i, 0)):
                    act.wait_ge(y_lo_ok.sem, y_lo_ok.at(i, 0))
                if type(i) is int and i == CHUNKS:
                    act.wait_ge(v_l.sem, 2)
                scaled_out(i, n, "b_a", gate[:, 0, :, 0:n], ACT.Sigmoid, sig_ok)
                prepare(0)
                if first:
                    act.wait_ge(kvp.sem, KT)
                    nc.scalar.activation(kv[:, :, :], sps[:, :, :], ACT.Copy).then_inc(kv_ok.sem, 2)
                if nxt:
                    squares(nxt[0][1], nxt[0][3], i)
                prepare(1)
                if first:
                    keys_values_hi(0)
                    act.wait_ge(pw_in.sem, 64)
                    nc.scalar.activation(pw_hi[:, :, :], ya[:, 0, :].rearrange("p (c m) -> p c m", c=CT), ACT.Copy).then_inc(pw_ok.sem, 1)
                scaled_out(i, n, "x_q", dq_hi[:, :, 0:n], ACT.Copy, q_hi)
                prepare(2)
                act.wait_ge(hist_ok.sem, hist_ok.at(i, 3))
                if needed(d_ok.at(i, 0)):
                    act.wait_ge(d_ok.sem, d_ok.at(i, 0))
                scaled_out(i, n, "c_u", cu[:, :, HP:HP + n], ACT.Copy, cu_ok)
                prepare(3)
                exps(i, n, 0)
                scaled_out(i, n, "a_c", gate[:, 1, :, 0:n], ACT.Copy, ac_ok)
                prepare(4)
                probs_hi(i, n, 0)
                exps(i, n, 1)
                prepare(5)
                act.wait_ge(d_ok.sem, d_ok.at(i, 1))
                act.wait_ge(s_ready.sem, s_ready.at(i, 2))
                nc.scalar.activation(dq_hi[:, :, 0:n], yc[:, :, 0:n], ACT.Copy).then_inc(d_hi.sem, 1)
                prepare(6)
                probs_hi(i, n, 1)
                scaled_out(i, n, "a_g", gate[:, 2, :, 0:n], ACT.Silu, ag_ok)
                prepare(7)
                act.wait_ge(d_lo.sem, d_lo.at(i, 1))
                u = at(i, "mix")
                for c in range(CT):
                    ins = nc.scalar.activation(yc[:, c, 0:n], u[:, c, 0:n], ACT.Identity,
                                               scale=cst[:, c, R_PS:R_PS + 1], bias=pbs[:, c:c + 1])
                ins.then_inc(mix_ok.sem, 1)
                act.wait_ge(glu_ok.sem, glu_ok.at(i, 1))
                scaled_out(i, n, "b_g", gate[:, 0, :, 0:n], ACT.Silu, bg_ok)
                y_high(i, n, 0, ya[:, :, 0:n], ya_ok)
                act.wait_ge(va_ok.sem, va_ok.at(i, 1))
                scaled_out(i, n, "c_g", gate[:, 1, :, 0:n], ACT.Silu, cg_ok)
                for q in range(WST):
                    piece_hi(i, q)
                scaled_out(i, n, "x_g", gate[:, 2, :, 0:n], ACT.Silu, xg_ok)
                y_high(i, n, 4, yc[:, :, 0:n], yc_ok)
                y_high(i, n, 6, gate[:, 2, :, 0:n], yx_ok)
                u = at(i, "zb")
                for c in range(CT):
                    ins = nc.scalar.activation(z[:, c, 0:n], u[:, c, 0:n], ACT.Silu,
                                               scale=cst[:, c, R_LNG:R_LNG + 1], bias=cst[:, c, R_LNB:R_LNB + 1])
                ins.then_inc(zs_ok.sem, 1)
                if nxt:
                    rows_hi(i, nxt[0][0], *nxt[0][1:])
                y_high(i, n, 2, z[:, :, 0:n], yb_ok)
                for q in range(WST, PIECES):
                    piece_hi(i, q)
                    if q == KT + 1 and len(nxt) > 1:
                        squares(nxt[1][1], nxt[1][3], i)
                    if type(i) is int and i == LAST and q == PIECES - 1:
                        keys_values_hi(1)
                    if q == KT + 7 and len(nxt) > 1:
                        rows_hi(i, nxt[1][0], *nxt[1][1:])
                nt = len(tiles(n))
                act.wait_ge(r_ok.sem, r_ok.at(i, 2 * nt))
                if needed(o_v.at(i, 0)):
                    act.wait_ge(o_v.sem, o_v.at(i, 0))
                for t, _, m in tiles(n):
                    if needed(o_sq.at(i, t)):
                        act.wait_ge(o_sq.sem, o_sq.at(i, t))
                    if nxt:
                        act.wait_ge(x_sq.sem, nxt[-1][1] + 1)
                    nc.scalar.activation(junk[0:m, :], ob[0:m, t, :], ACT.Square,
                                         accum_out=O_SQ[0:m, t:t + 1]).then_inc(o_sq.sem, 1)
                if type(i) is int and i >= LAST:
                    states_ok(i - LAST)

            act.wait_ge(ctr.sem, 1)
            nc.scalar.activation(cst[:, :, :], ops[:, 0:CT * NR].rearrange("p (c r) -> p c r", c=CT), ACT.Copy)
            nc.scalar.activation(gcol[:, :], ops[:, CT * NR:CT * NR + 2 * KT], ACT.Copy).then_inc(cev.sem, 1)
            squares(0, P, rows=ob[:, 0], loaded=first_in[0].sem)
            act.wait_ge(cev.sem, 1)
            rows_hi(0, ("t0", "t1"), 0, 0, P)
            squares(1, P, rows=ob[:, 1], loaded=first_in[1].sem)
            rows_hi(0, ("t2", "t3"), 1, 1, P)
            magnitudes(0)
            squares(2, P, loaded=first_in[2].sem)
            magnitudes(1)
            squares(3, P, rows=ob[:, 0], loaded=first_in[3].sem)
            w_high(0)
            memory_hi(0)
            for k in range(4):
                kw(k)
            magnitudes(2)
            memory_hi(1)
            w_high(1)
            magnitudes(3)
            for k in range(4, KT):
                kw(k)
            w_high(2)
            magnitudes(4)

            def next_tiles(i, names=("t0", "t1", "t2", "t3")):
                return [(names[0:2], 2 * i + 4, 0, P), (names[2:4], 2 * i + 5, 1, P)]

            chunk(0, N, next_tiles(0, ("n0", "n1", "n2", "n3")))
            with act.Fori(1, LAST) as i:
                chunk(i, N, next_tiles(i))
            chunk(LAST, N, [(("t0", "t1"), 2 * LAST + 4, 0, SAMPLE)])
            chunk(CHUNKS, SAMPLE, [])

        @block.vector
        def _(dve):
            def at(i, name):
                n, bank = slot(i, name)
                dve.wait_ge(u_ready.sem, n)
                return bank[:, :].rearrange("p (c n) -> p c n", c=CT)

            def rsqrt(s, i, k, sq, v, w, y, mul, add=EPS):
                if needed(s.at(i, k)):
                    dve.wait_ge(s.sem, s.at(i, k))
                nc.vector.tensor_scalar(w, sq, mul, add, ALU.mult, ALU.add).then_inc(s.sem, 1)
                nc.vector.tensor_scalar(v, sq, -0.5 * mul, -0.5 * add, ALU.mult, ALU.add).then_inc(s.sem, 1)
                dve.wait_ge(s.sem, s.at(i, k + 1))
                nc.vector.tensor_scalar(y.bitcast(I32), w.bitcast(I32), 1, None, ALU.logical_shift_right).then_inc(s.sem, 1)
                dve.wait_ge(s.sem, s.at(i, k + 3))
                nc.vector.tensor_scalar(y.bitcast(I32), y.bitcast(I32), -1.0, float(MAGIC), ALU.mult, ALU.add).then_inc(s.sem, 1)
                cols = y.shape[1]
                for r in range(2 * NEWTON):
                    for c in range(cols):
                        e = slice(c, c + 1)
                        dve.wait_ge(s.sem, s.at(i, k + 4 + max(0, (r - 1) * cols + c + 1)))
                        if r % 2 == 0:
                            nc.vector.scalar_tensor_tensor(w[:, e], y[:, e], v[:, e], y[:, e], ALU.mult, ALU.mult).then_inc(s.sem, 1)
                        else:
                            nc.vector.scalar_tensor_tensor(y[:, e], w[:, e], 1.5, y[:, e], ALU.add, ALU.mult).then_inc(s.sem, 1)

            def rows_rms(j, m):
                dve.wait_ge(x_sq.sem, j + 1)
                if needed(j):
                    dve.wait_ge(x_scaled.sem, j)
                rsqrt(x_v, 0, RSQRT * j, X_SQ[0:m, 0:1], X_V[0:m, 0:1], X_SH[0:m, 0:1], X_Y[0:m, 0:1], 1.0 / D)

            def rows_scale(j, m, factor, rows=xb):
                dve.wait_ge(x_v.sem, RSQRT * (j + 1))
                nc.vector.tensor_scalar(rows[0:m, :], rows[0:m, :], X_Y[0:m, 0:1], factor, ALU.mult, ALU.mult).then_inc(x_scaled.sem, 1)

            def rows_lo(i, names, hi_base, t, m):
                for h, name in enumerate(names):
                    n, bank = slot(i, name)
                    dve.wait_ge(h_hi_ok.sem, hi_base + h + 1)
                    src = bank[:, :].rearrange("p (k c) -> p k c", k=4)[:, :, 0:m]
                    o = (slice(None), slice(4 * h, 4 * h + 4), slice(t * P, t * P + m))
                    nc.vector.tensor_tensor(h_lo[o], src, h_hi[o], ALU.subtract).then_inc(h_lo_ok.sem, 1)

            def piece_lo(i, q):
                dve.wait_ge(wo_hi_ok.sem, wo_hi_ok.at(i, q + 1))
                nc.vector.tensor_tensor(wo_lo[:, q % WST, :], raws[q % RAW],
                                        wo_hi[:, q % WST, :].bitcast(F32), ALU.subtract).then_inc(wo_lo_ok.sem, 1)

            def w_scale(g):
                n, bank = slot(0, f"w{g}")
                b = 2 + g % 2
                dve.wait_ge(u_ready.sem, n)
                if needed(5 * g):
                    dve.wait_ge(l1_s.sem, 5 * g)
                nc.vector.tensor_scalar(l1[:, 0, :], bank[:, 0:CT * P], 2.0 ** -100, None, ALU.max).then_inc(l1_s.sem, 1)
                dve.wait_ge(l1_s.sem, 5 * g + 1)
                nc.vector.tensor_scalar(l1[:, 1, :].bitcast(I32), l1[:, 0, :].bitcast(I32), 0x7F800000, None,
                                        ALU.bitwise_and).then_inc(l1_s.sem, 1)
                if g >= 2:
                    dve.wait_ge(scaled1.sem, g - 1)
                dve.wait_ge(l1_s.sem, 5 * g + 2)
                nc.vector.tensor_scalar(l1[:, b, :].bitcast(I32), l1[:, 1, :].bitcast(I32), -1.0,
                                        float((WEXP + 254) << 23), ALU.mult, ALU.add).then_inc(l1_s.sem, 1)
                for c in range(CT):
                    o = slice(c * P, (c + 1) * P)
                    ins = nc.vector.scalar_tensor_tensor(l1[:, 0, o], l1[:, 1, o], 2.0 ** -WEXP / XSCALE, ident[:, :],
                                                         ALU.mult, ALU.mult)
                ins.then_inc(l1_s.sem, 1)
                dve.wait_ge(l1_s.sem, 5 * g + 4)
                nc.vector.reduce_sum(inv[:, CT * g:CT * g + CT], l1[:, 0, :].rearrange("p (c n) -> p c n", c=CT),
                                     axis=AX.X).then_inc(l1_s.sem, 1)
                dve.wait_ge(wg_ok.sem, CT * g + 1)
                dve.wait_ge(mags_ok.sem, CT * g + 1)
                nc.vector.tensor_tensor(w_raw(CT * g), w_raw(CT * g), l1[:, b, 0:P].unsqueeze(1).to_broadcast([P, KT, P]),
                                        ALU.mult).then_inc(scaled0.sem, 1)

            def w_low(g):
                dve.wait_ge(whi_ok.sem, CT * g + 1)
                if g:
                    dve.wait_ge(wlo1_ok.sem, g)
                nc.vector.tensor_tensor(w_lo[:, CT * g], w_raw(CT * g), w_hi[:, CT * g], ALU.subtract).then_inc(wlo0_ok.sem, 1)

            def taps(i, n, k0, k1):
                for k in range(k0, k1):
                    for c in range(CT):
                        w = cst[:, c, R_BW + k:R_BW + k + 1]
                        if k == 0:
                            ins = nc.vector.tensor_scalar(z[:, c, 0:n], glu[:, c, k:k + n], w,
                                                          cst[:, c, R_BIAS:R_BIAS + 1], ALU.mult, ALU.add)
                        else:
                            dve.wait_ge(conv_step.sem, conv_step.at(i, 2 * (k - 1) + c + 1))
                            ins = nc.vector.scalar_tensor_tensor(z[:, c, 0:n], glu[:, c, k:k + n], w, z[:, c, 0:n],
                                                                 ALU.mult, ALU.add)
                        ins.then_inc(conv_step.sem, 1)

            def softmax_max(i, n, p):
                nt = len(tiles(n))
                m = min(n, P)
                dve.wait_ge(s_ready.sem, s_ready.at(i, p + 1))
                nc.vector.reduce_max(nmax[0:m, p * nt:(p + 1) * nt, :].rearrange("p t h -> p h t"),
                                     sps[0:m, :, 0:nt * NMEM].rearrange("p h (t k) -> p h t k", k=NMEM),
                                     axis=AX.X, negate=True).then_inc(nmax_ok.sem, 1)

            def softmax_norm(i, n, p):
                nt = len(tiles(n))
                for t, t0, m in tiles(n):
                    s = p * nt + t
                    dve.wait_ge(exp_ok.sem, exp_ok.at(i, s + 1))
                    nc.vector.reciprocal(rcp[0:m, s, :], rsum[0:m, s, :]).then_inc(rcp_ok.sem, 1)
                for t, t0, m in tiles(n):
                    s = p * nt + t
                    dve.wait_ge(rcp_ok.sem, rcp_ok.at(i, s + 1))
                    for h in range(2):
                        ins = nc.vector.tensor_scalar(probs[0:m, s % 2, h, :], probs[0:m, s % 2, h, :],
                                                      rcp[0:m, s, h:h + 1], None, ALU.mult)
                    ins.then_inc(p_ok.sem, 1)

            def probs_lo(i, n, p):
                for h in range(2):
                    dve.wait_ge(pt_hi_ok.sem, pt_hi_ok.at(i, 2 * p + h + 1))
                    src = qps[:, h, :].rearrange("p (k n) -> p k n", k=MT)[:, :, 0:n]
                    nc.vector.tensor_tensor(pt_lo[:, h, :, 0:n], src, pt_hi[:, h, :, 0:n].bitcast(F32), ALU.subtract).then_inc(pt_lo_ok.sem, 1)

            def memory_lo(t):
                for h in range(2):
                    dve.wait_ge(mn_hi.sem, 2 * t + h + 1)
                    bank = mem_t[2 * t + h]
                    for k in range(4):
                        kk = 4 * h + k
                        ins = nc.vector.scalar_tensor_tensor(y_lo[:, kk, t * P:(t + 1) * P], bank[:, k * P:(k + 1) * P],
                                                             gcol[:, KT + kk:KT + kk + 1],
                                                             y_hi[:, kk, t * P:(t + 1) * P].bitcast(F32), ALU.mult, ALU.subtract)
                    ins.then_inc(mn_lo.sem, 1)

            def kw(k):
                b = k % 4
                dve.wait_ge(kw_hi.sem, k + 1)
                nc.vector.tensor_tensor(wo_lo[:, k % WST, :], raw[:, b, :],
                                        wo_hi[:, k % WST, :].bitcast(F32), ALU.subtract).then_inc(kw_lo.sem, 1)

            def chunk(i, n, nxt):
                first = type(i) is int and i == 0
                nt = len(tiles(n))

                def prepare(g):
                    if first:
                        w_low(g + AHEAD - 1)
                        if g + AHEAD < NG:
                            w_scale(g + AHEAD)

                if not first and not (type(i) is int and i == CHUNKS):
                    dve.wait_ge(win_ok.sem, win_ok.at(i, 0))
                    nc.vector.tensor_copy(glu[:, :, 0:HB], glu[:, :, N:N + HB]).then_inc(hist_ok.sem, 1)
                    nc.vector.tensor_copy(va[:, :, 0:HA], va[:, :, N:N + HA]).then_inc(hist_ok.sem, 1)
                    nc.vector.tensor_copy(cu[:, :, 0:HP], cu[:, :, N:N + HP]).then_inc(hist_ok.sem, 1)
                    dve.wait_ge(hist_ok.sem, hist_ok.at(i, 3))
                if not first and nxt:
                    normalise(i - 1, N)
                prepare(0)
                dve.wait_ge(sig_ok.sem, sig_ok.at(i, 1))
                u = at(i, "b_v")
                for c in range(CT):
                    f = pos("b_v") + c
                    ins = nc.vector.scalar_tensor_tensor(glu[:, c, HB:HB + n], u[:, c, 0:n], inv[:, f:f + 1],
                                                         gate[:, 0, c, 0:n], ALU.mult, ALU.mult)
                ins.then_inc(glu_ok.sem, 1)
                prepare(1)
                if first:
                    keys_values_lo(0)
                    dve.wait_ge(pw_ok.sem, 1)
                    nc.vector.tensor_tensor(pw_lo[:, :, :], ya[:, 0, :].rearrange("p (c m) -> p c m", c=CT),
                                            pw_hi[:, :, :].bitcast(F32), ALU.subtract).then_inc(pw_ok.sem, 1)
                dve.wait_ge(glu_ok.sem, glu_ok.at(i, 1))
                if needed(y_lo_ok.at(i, 0)):
                    dve.wait_ge(y_lo_ok.sem, y_lo_ok.at(i, 0))
                if nxt:
                    rows_rms(nxt[0][0], nxt[0][2])
                taps(i, n, 0, 6)
                dve.wait_ge(q_hi.sem, q_hi.at(i, 1))
                u = at(i, "x_q")
                for c in range(CT):
                    f = pos("x_q") + c
                    ins = nc.vector.scalar_tensor_tensor(dq_lo[:, c, 0:n], u[:, c, 0:n], inv[:, f:f + 1],
                                                         dq_hi[:, c, 0:n].bitcast(F32), ALU.mult, ALU.subtract)
                ins.then_inc(q_lo.sem, 1)
                prepare(2)
                prepare(3)
                taps(i, n, 6, 11)
                softmax_max(i, n, 0)
                if nxt:
                    rows_scale(nxt[0][0], nxt[0][2], XSCALE)
                taps(i, n, 11, 12)
                softmax_norm(i, n, 0)
                if not nxt:
                    normalise(i - 1, N)
                prepare(4)
                taps(i, n, 12, 18)
                probs_lo(i, n, 0)
                softmax_max(i, n, 1)
                taps(i, n, 18, 20)
                softmax_norm(i, n, 1)
                dve.wait_ge(win_ok.sem, win_ok.at(i, 4))
                if needed(yc_ok.at(i, 0)):
                    dve.wait_ge(yc_ok.sem, yc_ok.at(i, 0))
                for c in range(CT):
                    for h in range(2):
                        r = slice(h * HD, (h + 1) * HD)
                        sums = (sa[r, c, S2:S2 + n], sb_[r, c, S4:S4 + n])[h]
                        ins = nc.vector.scalar_tensor_tensor(yc[r, c, 0:n], sums, 1.0 / WINDOWS[2 * c + h],
                                                             cu[r, c, HP:HP + n], ALU.mult, ALU.subtract)
                ins.then_inc(d_ok.sem, 1)
                dve.wait_ge(ac_ok.sem, ac_ok.at(i, 1))
                u = at(i, "a_x")
                for c in range(CT):
                    f = pos("a_x") + c
                    ins = nc.vector.scalar_tensor_tensor(va[:, c, HA:HA + n], u[:, c, 0:n], inv[:, f:f + 1],
                                                         gate[:, 1, c, 0:n], ALU.mult, ALU.mult)
                ins.then_inc(va_ok.sem, 1)
                prepare(5)
                taps(i, n, 20, 22)
                dve.wait_ge(d_hi.sem, d_hi.at(i, 1))
                nc.vector.tensor_tensor(dq_lo[:, :, 0:n], yc[:, :, 0:n], dq_hi[:, :, 0:n].bitcast(F32), ALU.subtract).then_inc(d_lo.sem, 1)
                dve.wait_ge(va_ok.sem, va_ok.at(i, 1))
                if needed(y_lo_ok.at(i, 0)):
                    dve.wait_ge(y_lo_ok.sem, y_lo_ok.at(i, 0))
                if first:
                    dve.wait_ge(pw_ok.sem, 2)
                for k in range(TA):
                    for c in range(CT):
                        w = cst[:, c, R_AW + k:R_AW + k + 1]
                        if k == 0:
                            ins = nc.vector.tensor_scalar(ya[:, c, 0:n], va[:, c, k:k + n], w, None, ALU.mult)
                        else:
                            dve.wait_ge(conv_a.sem, conv_a.at(i, 2 * (k - 1) + c + 1))
                            ins = nc.vector.scalar_tensor_tensor(ya[:, c, 0:n], va[:, c, k:k + n], w, ya[:, c, 0:n],
                                                                 ALU.mult, ALU.add)
                        ins.then_inc(conv_a.sem, 1)
                taps(i, n, 22, 23)
                u = at(i, "a_b")
                for c in range(CT):
                    f = pos("a_b") + c
                    dve.wait_ge(conv_a.sem, conv_a.at(i, 2 * (TA - 1) + c + 1))
                    nc.vector.scalar_tensor_tensor(ya[:, c, 0:n], u[:, c, 0:n], inv[:, f:f + 1],
                                                   ya[:, c, 0:n], ALU.mult, ALU.mult).then_inc(conv_a.sem, 1)
                prepare(6)
                probs_lo(i, n, 1)
                taps(i, n, 23, TB)
                prepare(7)
                if needed(zt_ok.at(i, 0)):
                    dve.wait_ge(zt_ok.sem, zt_ok.at(i, 0))
                n_zf, bank = slot(i, "zf")
                dve.wait_ge(u_ready.sem, n_zf)
                for t, _, m in tiles(n):
                    ins = nc.vector.bn_stats(bn6[0:m, t, :], bank[0:m, t * GW:(t + 1) * GW])
                ins.then_inc(bn_s.sem, 1)
                dve.wait_ge(bn_s.sem, bn_s.at(i, 1))
                dve.wait_ge(ag_ok.sem, ag_ok.at(i, 1))
                dve.wait_ge(conv_a.sem, conv_a.at(i, 4 * CT))
                nc.vector.tensor_tensor(ya[:, :, 0:n], ya[:, :, 0:n], gate[:, 2, :, 0:n], ALU.mult).then_inc(ya_ok.sem, 1)
                for t, _, m in tiles(n):
                    ins = nc.vector.bn_aggr(mv[0:m, t, :], bn6[0:m, t, :])
                ins.then_inc(bn_s.sem, 1)
                dve.wait_ge(bn_s.sem, bn_s.at(i, 2))
                m0 = min(n, P)
                rsqrt(ln_v, i, 0, mv[0:m0, 0:nt, 1], L_V[0:m0, 0:nt], L_SH[0:m0, 0:nt], L_Y[0:m0, 0:nt], 1.0)
                dve.wait_ge(ln_v.sem, ln_v.at(i, 4 + 2 * NEWTON * nt))
                for t, _, m in tiles(n):
                    ins = nc.vector.tensor_scalar(zt[0:m, t, :], bank[0:m, t * GW:(t + 1) * GW], mv[0:m, t, 0:1],
                                                  L_Y[0:m, t:t + 1], ALU.subtract, ALU.mult)
                ins.then_inc(zt_ok.sem, 1)
                for q in range(WST):
                    piece_lo(i, q)
                dve.wait_ge(xg_ok.sem, xg_ok.at(i, 1))
                dve.wait_ge(pv_ready.sem, pv_ready.at(i, 2))
                nc.vector.tensor_tensor(gate[:, 2, :, 0:n], ops[:, :].rearrange("p (c n) -> p c n", c=CT)[:, :, 0:n],
                                        gate[:, 2, :, 0:n], ALU.mult).then_inc(yx_ok.sem, 1)
                dve.wait_ge(zs_ok.sem, zs_ok.at(i, 1))
                dve.wait_ge(bg_ok.sem, bg_ok.at(i, 1))
                nc.vector.tensor_tensor(z[:, :, 0:n], z[:, :, 0:n], gate[:, 0, :, 0:n], ALU.mult).then_inc(yb_ok.sem, 1)
                if nxt:
                    rows_lo(i, nxt[0][4], nxt[0][1], 0, nxt[0][2])
                for q in range(WST, PIECES):
                    piece_lo(i, q)
                    if q == KT + 2 and len(nxt) > 1:
                        rows_rms(nxt[1][0], nxt[1][2])
                    if q == KT + 5 and len(nxt) > 1:
                        rows_scale(nxt[1][0], nxt[1][2], XSCALE)
                    if q == KT + 3:
                        add_half(i, n, 0)
                    if type(i) is int and i == LAST and q == PIECES - 1:
                        keys_values_lo(1)
                    if q == KT + 7 and len(nxt) > 1:
                        rows_lo(i, nxt[1][4], nxt[1][1], 1, nxt[1][2])
                add_half(i, n, 1)

            def normalise(i, n):
                nt, m0 = len(tiles(n)), min(n, P)
                dve.wait_ge(o_sq.sem, o_sq.at(i, nt))
                if needed(o_ok.at(i, 0)):
                    dve.wait_ge(o_ok.sem, o_ok.at(i, 0))
                rsqrt(o_v, i, 0, O_SQ[0:m0, 0:nt], O_V[0:m0, 0:nt], O_SH[0:m0, 0:nt], O_Y[0:m0, 0:nt], 1.0 / D)
                dve.wait_ge(gf_in.sem, 16)
                dve.wait_ge(o_v.sem, o_v.at(i, 4 + 2 * NEWTON * nt))
                for t, _, m in tiles(n):
                    ins = nc.vector.scalar_tensor_tensor(ob[0:m, t, :], ob[0:m, t, :], O_Y[0:m, t:t + 1], gf[0:m, :],
                                                         ALU.mult, ALU.mult)
                ins.then_inc(o_ok.sem, 1)

            def add_half(i, n, half):
                banks = sps if half == 0 else qps
                dve.wait_ge(o_piece.sem, o_piece.at(i, (half + 1) * KT))
                for t, _, m in tiles(n):
                    if half == 0:
                        dve.wait_ge(res_in[t].sem, res_in[t].at(i, 16))
                    c = slice(half * HALF, (half + 1) * HALF)
                    nc.vector.tensor_tensor(ob[0:m, t, c], banks[0:m, t, :], ob[0:m, t, c], ALU.add).then_inc(r_ok.sem, 1)

            def keys_values_lo(k):
                dve.wait_ge(kt_h.sem, k + 1)
                nc.vector.scalar_tensor_tensor(kt_lo[:, :, :], ops[:, :].rearrange("p (a m) -> p a m", a=PAIRS),
                                               HD ** -0.5, kt_hi[:, :, :].bitcast(F32), ALU.mult, ALU.subtract).then_inc(kt_l.sem, 1)
                dve.wait_ge(v_h.sem, k + 1)
                for t in range(MT):
                    src = (kv, kv_s)[k][:, t, GW:2 * GW].rearrange("p (a h d) -> p a h d", a=PAIRS, h=2)
                    hi = v_hi[:, t].rearrange("p a (s d) -> p a s d", s=3)[:, :, 0::2, :]
                    lo = v_lo[:, t].rearrange("p a (s d) -> p a s d", s=3)[:, :, 0::2, :]
                    ins = nc.vector.tensor_tensor(lo, src, hi.bitcast(F32), ALU.subtract)
                ins.then_inc(v_l.sem, 1)

            nc.vector.memset(ya[:, 0, :], 0.0).then_inc(zero_ok.sem, 1)
            for buf in (glu[:, :, 0:HB], va[:, :, 0:HA], cu[:, :, 0:HP]):
                nc.vector.memset(buf, 0.0).then_inc(hist_ok.sem, 1)
            for buf in (v_hi, v_lo):
                nc.vector.memset(buf[:, :, :, HD:2 * HD].bitcast(F32), 0.0).then_inc(zero_ok.sem, 1)
            dve.wait_ge(ramp_s.sem, 2)
            for c in range(CT):
                for h in range(2):
                    r = slice(h * HD, (h + 1) * HD)
                    ins = nc.vector.tensor_scalar(ramp[r, c, :], ramp[r, c, :], float(WINDOWS[2 * c + h]),
                                                  1.0 / WINDOWS[2 * c + h], ALU.min, ALU.mult)
            ins.then_inc(ramp_s.sem, 1)
            dve.wait_ge(ramp_s.sem, 3)
            nc.vector.reciprocal(ramp[:, :, :], ramp[:, :, :]).then_inc(ramp_s.sem, 1)
            dve.wait_ge(cev.sem, 1)
            nc.vector.tensor_tensor(pbs[:, :], cst[:, :, R_PB], cst[:, :, R_PS], ALU.mult).then_inc(consts_ok.sem, 1)
            rows_rms(0, P)
            rows_scale(0, P, XSCALE, ob[:, 0])
            rows_lo(0, ("t0", "t1"), 0, 0, P)
            rows_rms(1, P)
            rows_scale(1, P, XSCALE, ob[:, 1])
            rows_lo(0, ("t2", "t3"), 2, 1, P)
            w_scale(0)
            rows_rms(2, P)
            rows_scale(2, P, 1.0)
            w_scale(1)
            rows_rms(3, P)
            rows_scale(3, P, 1.0, ob[:, 0])
            w_low(0)
            memory_lo(0)
            for k in range(4):
                kw(k)
            w_scale(2)
            memory_lo(1)
            w_low(1)
            w_scale(3)
            for k in range(4, KT):
                kw(k)
            w_low(2)

            def next_tiles(i, names=("t0", "t1", "t2", "t3")):
                return [(2 * i + 4, 4 * i + 4, P, 0, names[0:2]), (2 * i + 5, 4 * i + 6, P, 1, names[2:4])]

            chunk(0, N, next_tiles(0, ("n0", "n1", "n2", "n3")))
            with dve.Fori(1, LAST) as i:
                chunk(i, N, next_tiles(i))
            chunk(LAST, N, [(2 * LAST + 4, 4 * LAST + 4, SAMPLE, 0, ("t0", "t1"))])
            dve.wait_ge(stp.sem, 2)
            for c in range(CT):
                nc.vector.tensor_copy(glu[:, c, 0:HB], ops[:, c * P:c * P + HB])
                nc.vector.tensor_copy(cu[:, c, 0:HP], ops[:, c * P + 32:c * P + 32 + HP])
                ins = nc.vector.tensor_copy(va[:, c, 0:HA], ops[:, c * P + 64:c * P + 64 + HA])
            ins.then_inc(hist_ok.sem, 3)
            dve.wait_ge(hist_ok.sem, hist_ok.at(CHUNKS, 3))
            dve.wait_ge(stored_st.sem, 48)
            chunk(CHUNKS, SAMPLE, [])
            normalise(CHUNKS, SAMPLE)

        @block.gpsimd
        def _(pool):
            def w_gain(g):
                pool.wait_ge(w_in_ok[g].sem, 16 * CT)
                for j in (CT * g, CT * g + 1):
                    nc.gpsimd.tensor_tensor(w_raw(j), w_raw(j), gcol[:, 0:KT].unsqueeze(2).to_broadcast([P, KT, P]),
                                            ALU.mult).then_inc(wg_ok.sem, 1)

            def w_scale1(g):
                j = CT * g + 1
                pool.wait_ge(l1_s.sem, 5 * g + 3)
                pool.wait_ge(mags_ok.sem, j + 1)
                nc.gpsimd.tensor_tensor(w_raw(j), w_raw(j), l1[:, 2 + g % 2, P:2 * P].unsqueeze(1).to_broadcast([P, KT, P]),
                                        ALU.mult).then_inc(scaled1.sem, 1)

            def w_low1(g):
                j = CT * g + 1
                pool.wait_ge(whi_ok.sem, j + 1)
                nc.gpsimd.tensor_tensor(w_lo[:, j], w_raw(j), w_hi[:, j], ALU.subtract).then_inc(wlo1_ok.sem, 1)

            def y_low(i, n, k, src, a):
                pool.wait_ge(y_hi_ok.sem, y_hi_ok.at(i, a + 1))
                nc.gpsimd.tensor_tensor(y_lo[:, k:k + CT, 0:n], src, y_hi[:, k:k + CT, 0:n].bitcast(F32),
                                        ALU.subtract).then_inc(y_lo_ok.sem, 1)

            def chunk(i, n):
                first = type(i) is int and i == 0

                def prepare(g):
                    if first:
                        w_scale1(g + AHEAD - 1)
                        if g + GAINS < NG:
                            w_gain(g + GAINS)
                        w_low1(g + AHEAD - 1)

                prepare(0)
                prepare(1)
                prepare(2)
                prepare(3)
                pool.wait_ge(cu_ok.sem, cu_ok.at(i, 1))
                if needed(zs_ok.at(i, 0)):
                    pool.wait_ge(zs_ok.sem, zs_ok.at(i, 0))
                nc.gpsimd.tensor_tensor(sa[:, :, 0:S2 + n], cu[:, :, 1:HP + n], cu[:, :, 0:HP + n - 1], ALU.add).then_inc(win_ok.sem, 1)
                pool.wait_ge(win_ok.sem, win_ok.at(i, 1))
                nc.gpsimd.tensor_tensor(sb_[:, :, 0:S4 + n], sa[:, :, 2:S2 + n], sa[:, :, 0:S2 + n - 2], ALU.add).then_inc(win_ok.sem, 1)
                pool.wait_ge(win_ok.sem, win_ok.at(i, 2))
                nc.gpsimd.tensor_tensor(sa[:, 1, 6:S2 + n], sb_[:, 1, 4:S4 + n], sb_[:, 1, 0:S4 + n - 4], ALU.add).then_inc(win_ok.sem, 1)
                pool.wait_ge(win_ok.sem, win_ok.at(i, 3))
                r = slice(HD, P)
                last = nc.gpsimd.tensor_tensor(sb_[r, 1, S4:S4 + n], sa[r, 1, S2:S2 + n], sa[r, 1, S2 - 8:S2 + n - 8], ALU.add)
                if first:
                    last.then_inc(ramp_s.sem, 1)
                    pool.wait_ge(ramp_s.sem, 5)
                    nc.gpsimd.tensor_tensor(sa[0:HD, :, S2:S2 + 16], sa[0:HD, :, S2:S2 + 16], ramp[0:HD], ALU.mult)
                    last = nc.gpsimd.tensor_tensor(sb_[r, :, S4:S4 + 16], sb_[r, :, S4:S4 + 16], ramp[r], ALU.mult)
                last.then_inc(win_ok.sem, 1)
                pool.wait_ge(win_ok.sem, win_ok.at(i, 4))
                for g in range(4, 8):
                    prepare(g)
                y_low(i, n, 0, ya[:, :, 0:n], 0)
                pool.wait_ge(cg_ok.sem, cg_ok.at(i, 1))
                pool.wait_ge(mix_ok.sem, mix_ok.at(i, 1))
                nc.gpsimd.tensor_tensor(yc[:, :, 0:n], yc[:, :, 0:n], gate[:, 1, :, 0:n], ALU.mult).then_inc(yc_ok.sem, 1)
                pool.wait_ge(yc_ok.sem, yc_ok.at(i, 1))
                y_low(i, n, 4, yc[:, :, 0:n], 1)
                y_low(i, n, 6, gate[:, 2, :, 0:n], 2)
                y_low(i, n, 2, z[:, :, 0:n], 3)

            nc.gpsimd.memset(ident[:, :], 0.0).then_inc(ident_ok.sem, 1)
            nc.gpsimd.memset(ones[:, :], 1.0)
            pool.wait_ge(ident_ok.sem, 1)
            nc.gpsimd.affine_select(out=ident[:, :], in_=ident[:, :], compare_op=ALU.not_equal, fill=1.0, base=0,
                                    pattern=[[-1, P]], channel_multiplier=1).then_inc(ident_ok.sem, 1)
            nc.gpsimd.iota(l1[:, 0, 0:32].rearrange("p (c t) -> p c t", c=CT).bitcast(I32), [[0, CT], [1, 16]], base=1,
                           channel_multiplier=0).then_inc(ramp_s.sem, 1)
            pool.wait_ge(ramp_s.sem, 1)
            nc.gpsimd.tensor_copy(ramp[:, :, :], l1[:, 0, 0:32].rearrange("p (c t) -> p c t", c=CT).bitcast(I32)).then_inc(ramp_s.sem, 1)
            pool.wait_ge(cev.sem, 1)
            w_gain(0)
            w_gain(1)
            w_scale1(0)
            w_gain(2)
            w_low1(0)
            w_scale1(1)
            w_gain(3)
            w_low1(1)
            w_gain(4)
            w_scale1(2)
            w_low1(2)
            chunk(0, N)
            with pool.Fori(1, LAST) as i:
                chunk(i, N)
            chunk(LAST, N)
            chunk(CHUNKS, SAMPLE)


_INS = ["x_prompt", "x_sample", "mem_prompt", "state_conv_a", "state_conv_b", "state_pool", "cache_mem_k",
        "cache_mem_v", "norm_g", "w_in", "conv_a_w", "conv_b_w", "conv_b_bias", "ln_b_g", "ln_b_b", "pool_w",
        "pool_bias", "pool_scale", "mem_norm_g", "w_mem_k", "w_mem_v", "w_out", "final_norm_g"]
_OUTS = [(1, SEQ, D), (1, SAMPLE, D), (1, 1, HA, GW), (1, 1, HB, GW), (1, 1, HP, GW),
         (1, 1, NMEM, HEADS, HD), (1, 1, NMEM, HEADS, HD), (1, 1, HA, GW), (1, 1, HB, GW), (1, 1, HP, GW)]


def kernel(**inputs):
    import numpy as np
    import concourse.bacc as bacc
    from concourse.bass_utils import run_bass_kernel_spmd

    nc = bacc.Bacc("TRN2", target_bir_lowering=False, num_devices=1)
    arrays, args = {}, []
    for name in _INS:
        a = np.ascontiguousarray(inputs[name])
        arrays[f"in_{name}"] = a
        args.append(nc.dram_tensor(f"in_{name}", a.shape, mybir.dt.from_np(a.dtype), kind="ExternalInput").ap())
    for k, shape in enumerate(_OUTS):
        args.append(nc.dram_tensor(f"out_{k}", shape, F32, kind="ExternalOutput").ap())
    encoder_program(nc, *args)
    r = run_bass_kernel_spmd(nc, [arrays], core_ids=[0])
    return tuple(r.results[0][f"out_{k}"] for k in range(len(_OUTS)))
```
